# Optimizing a Trainium2 kernel written in Bass

```python
import math
import jax, jax.numpy as jnp
from jax import lax
import numpy as np

D_MODEL = 1024
BATCH = 1
SEQ = 1024
DEPTH = 2

N_META = 16
CHUNK = 64
Q_BLOCK = 128
MIX_WIDTH = D_MODEL
LRU_WIDTH = MIX_WIDTH // 2
LRU_BLOCKS = 8
LRU_BLOCK_DIM = LRU_WIDTH // LRU_BLOCKS
LRU_CONV = 4
LRU_C = 8.0
ATT_WIDTH = MIX_WIDTH - LRU_WIDTH
DIFF_HEADS = 4
DIFF_HEAD_DIM = ATT_WIDTH // (2 * DIFF_HEADS)
V_HEAD_DIM = 2 * DIFF_HEAD_DIM
ROPE_THETA = 10000.0
D_FF = 3 * D_MODEL
FFN_CONV = 3
NORM_EPS = 1e-6
SUBLN_EPS = 1e-5
IN_WIDTH = 2 * LRU_WIDTH + 3 * ATT_WIDTH
NEG_INF = -1e30

kernel_name = "hymba_rglru_diffattn_convffn"

def rms_norm(x, g, eps=NORM_EPS):
    xf = x.astype(jnp.float32)
    y = xf * lax.rsqrt(jnp.mean(xf * xf, axis=-1, keepdims=True) + eps)
    return (y * g.astype(jnp.float32)).astype(x.dtype)

def causal_depthwise_conv(x, w, b):
    K = w.shape[0]
    T = x.shape[1]
    xp = jnp.pad(x, ((0, 0), (K - 1, 0), (0, 0)))
    y = b
    for k in range(K):
        y = y + xp[:, k:k + T, :] * w[k]
    return y

def rope_tables(T, dim):
    inv = 1.0 / (ROPE_THETA ** (jnp.arange(0, dim, 2, dtype=jnp.float32) / dim))
    ang = jnp.arange(T, dtype=jnp.float32)[:, None] * inv[None, :]
    return jnp.cos(ang), jnp.sin(ang)

def apply_rope(x, cos, sin):
    x1, x2 = jnp.split(x, 2, axis=-1)
    c = cos.astype(x.dtype)
    s = sin.astype(x.dtype)
    return jnp.concatenate([x1 * c - x2 * s, x2 * c + x1 * s], axis=-1)

def chunk_ids(T_pad, T):
    p = jnp.arange(T_pad, dtype=jnp.int32)
    cid = jnp.where(p < N_META, 0, 1 + (p - N_META) // CHUNK)
    return jnp.where(p < T, cid, jnp.iinfo(jnp.int32).max).astype(jnp.int32)

def rg_lru(x, wa, ba, wx, bx, a_param):
    B, T, _ = x.shape
    xb = x.reshape(B, T, LRU_BLOCKS, LRU_BLOCK_DIM)
    r = jax.nn.sigmoid(jnp.einsum('btnc,ncd->btnd', xb, wa) + ba).reshape(B, T, LRU_WIDTH)
    i = jax.nn.sigmoid(jnp.einsum('btnc,ncd->btnd', xb, wx) + bx).reshape(B, T, LRU_WIDTH)
    log_a = LRU_C * r.astype(jnp.float32) * jax.nn.log_sigmoid(a_param.astype(jnp.float32))
    a = jnp.exp(log_a)
    mult = jnp.sqrt(-jnp.expm1(2.0 * log_a))
    bterm = mult * (i * x).astype(jnp.float32)

    def combine(left, right):
        a1, b1 = left
        a2, b2 = right
        return a1 * a2, a2 * b1 + b2

    _, h = lax.associative_scan(combine, (a, bterm), axis=1)
    return h.astype(x.dtype)

def diff_attention(q, k, v, lam_q1, lam_k1, lam_q2, lam_k2, subln, lambda_init):
    B, T, _ = q.shape
    T_pad = -(-T // Q_BLOCK) * Q_BLOCK
    n_blk = T_pad // Q_BLOCK
    pad = T_pad - T
    q = q.reshape(B, T, DIFF_HEADS, 2, DIFF_HEAD_DIM).transpose(3, 0, 2, 1, 4)
    k = k.reshape(B, T, DIFF_HEADS, 2, DIFF_HEAD_DIM).transpose(3, 0, 2, 1, 4)
    v = v.reshape(B, T, DIFF_HEADS, V_HEAD_DIM).transpose(0, 2, 1, 3)
    cos, sin = rope_tables(T, DIFF_HEAD_DIM)
    q = apply_rope(q, cos, sin) * (DIFF_HEAD_DIM ** -0.5)
    k = apply_rope(k, cos, sin)
    q = jnp.pad(q, ((0, 0), (0, 0), (0, 0), (0, pad), (0, 0)))
    k = jnp.pad(k, ((0, 0), (0, 0), (0, 0), (0, pad), (0, 0)))
    v = jnp.pad(v, ((0, 0), (0, 0), (0, pad), (0, 0)))
    cid = chunk_ids(T_pad, T)
    lam = (jnp.exp(jnp.sum(lam_q1.astype(jnp.float32) * lam_k1.astype(jnp.float32)))
           - jnp.exp(jnp.sum(lam_q2.astype(jnp.float32) * lam_k2.astype(jnp.float32)))
           + lambda_init)
    qb = q.reshape(2, B, DIFF_HEADS, n_blk, Q_BLOCK, DIFF_HEAD_DIM).transpose(3, 0, 1, 2, 4, 5)
    cb = cid.reshape(n_blk, Q_BLOCK)

    def block(args):
        qi, ci = args
        s = jnp.einsum('mbhqd,mbhkd->mbhqk', qi, k).astype(jnp.float32)
        mask = cid[None, :] <= ci[:, None]
        s = jnp.where(mask, s, NEG_INF)
        p = jax.nn.softmax(s, axis=-1)
        w = p[0] - lam * p[1]
        return jnp.einsum('bhqk,bhke->bhqe', w.astype(v.dtype), v)

    o = lax.map(block, (qb, cb))
    o = o.transpose(1, 2, 0, 3, 4).reshape(B, DIFF_HEADS, T_pad, V_HEAD_DIM)[:, :, :T]
    o = rms_norm(o, subln, SUBLN_EPS) * (1.0 - lambda_init)
    return o.transpose(0, 2, 1, 3).reshape(B, T, ATT_WIDTH)

def setup_inputs(seed: int = 0) -> dict:
    key = jax.random.key(seed)
    ks = jax.random.split(key, 26)
    f32 = jnp.float32
    L = DEPTH

    def nrm(k, shape, scale):
        return jax.random.normal(k, shape, f32) * scale

    def gain(k, shape):
        return 1.0 + 0.02 * jax.random.normal(k, shape, f32)

    u = jax.random.uniform(ks[13], (L, LRU_WIDTH), f32, 0.9, 0.999)
    s = u ** (1.0 / LRU_C)
    a_param = jnp.log(s) - jnp.log1p(-s)
    return {
        "x": nrm(ks[0], (BATCH, SEQ, D_MODEL), 1.0),
        "meta_tokens": nrm(ks[1], (N_META, D_MODEL), 1.0),
        "ln_mix_pre": gain(ks[2], (L, D_MODEL)),
        "ln_mix_post": gain(ks[3], (L, D_MODEL)),
        "ln_ffn_pre": gain(ks[4], (L, D_MODEL)),
        "ln_ffn_post": gain(ks[5], (L, D_MODEL)),
        "w_in": nrm(ks[6], (L, D_MODEL, IN_WIDTH), D_MODEL ** -0.5),
        "lru_conv_w": nrm(ks[7], (L, LRU_CONV, LRU_WIDTH), LRU_CONV ** -0.5),
        "lru_conv_b": nrm(ks[8], (L, LRU_WIDTH), 0.01),
        "lru_wa": nrm(ks[9], (L, LRU_BLOCKS, LRU_BLOCK_DIM, LRU_BLOCK_DIM), LRU_BLOCK_DIM ** -0.5),
        "lru_ba": nrm(ks[10], (L, LRU_BLOCKS, LRU_BLOCK_DIM), 0.01),
        "lru_wx": nrm(ks[11], (L, LRU_BLOCKS, LRU_BLOCK_DIM, LRU_BLOCK_DIM), LRU_BLOCK_DIM ** -0.5),
        "lru_bx": nrm(ks[12], (L, LRU_BLOCKS, LRU_BLOCK_DIM), 0.01),
        "lru_a_param": a_param,
        "lru_out_norm": gain(ks[14], (L, LRU_WIDTH)),
        "lam_q1": nrm(ks[15], (L, DIFF_HEAD_DIM), 0.1),
        "lam_k1": nrm(ks[16], (L, DIFF_HEAD_DIM), 0.1),
        "lam_q2": nrm(ks[17], (L, DIFF_HEAD_DIM), 0.1),
        "lam_k2": nrm(ks[18], (L, DIFF_HEAD_DIM), 0.1),
        "diff_subln": gain(ks[19], (L, V_HEAD_DIM)),
        "w_out": nrm(ks[20], (L, MIX_WIDTH, D_MODEL), MIX_WIDTH ** -0.5),
        "w_up": nrm(ks[21], (L, D_MODEL, 2 * D_FF), D_MODEL ** -0.5),
        "ffn_conv_w": nrm(ks[22], (L, FFN_CONV, D_FF), FFN_CONV ** -0.5),
        "ffn_conv_b": nrm(ks[23], (L, D_FF), 0.01),
        "w_down": nrm(ks[24], (L, D_FF, D_MODEL), D_FF ** -0.5),
    }

def reference(x, meta_tokens, ln_mix_pre, ln_mix_post, ln_ffn_pre, ln_ffn_post, w_in,
              lru_conv_w, lru_conv_b, lru_wa, lru_ba, lru_wx, lru_bx, lru_a_param,
              lru_out_norm, lam_q1, lam_k1, lam_q2, lam_k2, diff_subln, w_out,
              w_up, ffn_conv_w, ffn_conv_b, w_down):
    B = x.shape[0]
    meta = jnp.broadcast_to(meta_tokens[None].astype(x.dtype), (B, N_META, D_MODEL))
    h = jnp.concatenate([meta, x], axis=1)
    splits = [LRU_WIDTH, 2 * LRU_WIDTH, 2 * LRU_WIDTH + ATT_WIDTH, 2 * LRU_WIDTH + 2 * ATT_WIDTH]
    for l in range(DEPTH):
        lambda_init = 0.8 - 0.6 * math.exp(-0.3 * l)
        u = rms_norm(h, ln_mix_pre[l])
        z = u @ w_in[l]
        xr, gr, q, k, v = jnp.split(z, splits, axis=-1)
        xr = causal_depthwise_conv(xr, lru_conv_w[l], lru_conv_b[l])
        hr = rg_lru(xr, lru_wa[l], lru_ba[l], lru_wx[l], lru_bx[l], lru_a_param[l])
        yr = rms_norm(hr * jax.nn.gelu(gr), lru_out_norm[l])
        ya = diff_attention(q, k, v, lam_q1[l], lam_k1[l], lam_q2[l], lam_k2[l],
                            diff_subln[l], lambda_init)
        y = jnp.concatenate([yr, ya], axis=-1) @ w_out[l]
        h = h + rms_norm(y, ln_mix_post[l])
        u = rms_norm(h, ln_ffn_pre[l])
        g, val = jnp.split(u @ w_up[l], 2, axis=-1)
        g = causal_depthwise_conv(g, ffn_conv_w[l], ffn_conv_b[l])
        f = (jax.nn.gelu(g) * val) @ w_down[l]
        h = h + rms_norm(f, ln_ffn_post[l])
    return h[:, N_META:]


_drawn_inputs = setup_inputs


def setup_inputs(seed=0):
    import zlib

    import numpy as np

    out = dict(_drawn_inputs(seed))
    spreads = {}
    factors = {'ln_ffn_post': 3.368,
     'lru_ba': 28.223,
     'lru_bx': 8.0,
     'lru_out_norm': 10.381,
     'lam_q2': 2.746,
     'diff_subln': 13.201,
     'ffn_conv_b': 6.987}
    for name, (base, spread) in spreads.items():
        noise = np.random.default_rng([zlib.crc32(name.encode()), seed]).standard_normal(out[name].shape)
        drawn = base * np.exp(spread * noise) if base else spread * noise
        out[name] = __import__('jax').numpy.asarray(drawn.astype(out[name].dtype))
    for name, factor in factors.items():
        out[name] = (out[name] * factor).astype(out[name].dtype)
    return out
```

```python
import concourse.bass as bass
from concourse import mybir
from contextlib import ExitStack

F32 = mybir.dt.float32
F32R = mybir.dt.float32r
ACT = mybir.ActivationFunctionType
ALU = mybir.AluOpType
AX_X = mybir.AxisListType.X

P = 128
L, D, SEQ, META = 2, 1024, 1024, 16
DC = D // P
TOK = META + SEQ
NT, TW = 3, 348
T = NT * TW
LRU_CH, HEADS, DH = 4, 4, 64
IN_W = 2560
FF, FC = 3072, 24
G = 2
NG = FC // G
NQ = 9
TILES = 3 * LRU_CH + 3 * HEADS + DC + FC * 3
BF = DC * T * 4

MIX_PRE, MIX_POST, FFN_PRE, FFN_POST = 0, 8, 16, 24
CONV_W, CONV_B, GATE_BA, GATE_BX, A_PAR, OUT_NORM, SUBLN, LAM = 32, 48, 52, 56, 60, 64, 68, 69
FCONV_W, FCONV_B = 128, 128 + 72
NEG_C, NPAR = 224, 256
POS_C, NEG_LAM, HEAD_GAIN = 228, 232, 233


class Steps:

    def __init__(self, sem, names):
        self.sem, self.names, self.n = sem, names, 0

    def inc(self, name):
        assert self.names[self.n % len(self.names)] == name, (name, self.names[self.n % len(self.names)])
        self.n += 1
        return self.sem, 1

    def at(self, name, k):
        return self.sem, k * len(self.names) + (2 * len(self.names) + self.names.index(name) + 1)


def trunk(nc, t, out):
    ctx = ExitStack()
    with ctx:
        base = (nc.sbuf_base + 63) // 64 * 64

        def at(name, off, shape, dt=F32):
            return nc.alloc_sbuf_tensor_at(name, [P, *shape], dt, offset=base + off)

        HH = at("h_hi", 0, [DC, T], F32R)
        HL = at("h_lo", BF, [DC, T], F32R)
        ACC = at("acc", 2 * BF, [DC, T])
        o = 3 * BF
        RAW = [at(f"raw{i}", o + 4096 * i, [DC, P]) for i in range(2)]
        o += 8192
        SLOT = o
        WH = [at(f"w_hi{i}", SLOT + 8192 * i, [DC, P], F32R) for i in range(4)]
        WL = [at(f"w_lo{i}", SLOT + 8192 * i + 4096, [DC, P], F32R) for i in range(4)]
        BDH = at("bd_hi", SLOT + 16384, [2, P], F32R)
        BDL = at("bd_lo", SLOT + 16384 + 1024, [2, P], F32R)
        VH = at("v_hi", SLOT + 16384, [NQ, P], F32R)
        VL = at("v_lo", SLOT + 16384 + 4608, [NQ, P], F32R)
        PTH = at("pt_hi", SLOT + 16384 + 9216, [NQ, P], F32R)
        o += 32768
        REG = o
        FH = at("f_hi", REG, [4, T], F32R)
        FL = at("f_lo", REG + 4 * T * 4, [4, T], F32R)
        HRES = at("h_res", REG, [DC, T])
        Lb = [HRES[:, i, :] for i in range(DC)]
        XPAD = at("x_pad", REG, [T + 3])
        XC = at("x_conv", REG + 4192, [T])
        XH = at("x_hi", REG + 8384, [T], F32R)
        XL = at("x_lo", REG + 12576, [T], F32R)
        GG = at("gate", REG + 16768, [T])
        RA = at("r_a", REG + 20960, [T])
        IB = at("i_b", REG + 25152, [T])
        QS = at("q_stack", REG, [2, T], F32R)
        KH = at("k_hi", REG + 8352, [2, T], F32R)
        KL = at("k_lo", REG + 16704, [2, T], F32R)
        PTL = at("pt_lo", REG + 25056, [NQ, P], F32R)
        o += BF
        S = [at(f"s{i}", o + 4192 * i, [T + 4]) for i in range(4)]
        XIN = [at(f"x_in{i}", o + 4192 * i, [D]) for i in range(2)]
        SQ8 = at("sq8", o + 8384, [DC, P])
        ROWS = at("rows", 2 * BF, [L, 2, P])
        OUTB = [at(f"out{i}", o + 4192 * i, [D]) for i in range(2)]
        o += 4 * 4192
        RSTD = at("rstd", o, [T]); o += 4192
        COS = at("cos", o, [T]); o += 4192
        SIN = at("sin", o, [T]); o += 4192
        IDENT = at("ident", o, [P]); o += 512
        ONES = at("ones", o, [P]); o += 512
        MASK = at("mask", o, [64]); o += 256
        BD = at("bd_raw", o, [2, P]); o += 1024
        PAR = at("par", o, [L, NPAR]); o += L * NPAR * 4
        CUR = at("cur", o, [NPAR]); o += NPAR * 4
        SM = at("small", o, [64]); o += 256
        CST = at("cst", o, [8]); o += 64
        assert base + o <= nc.sbuf_usable_end, (base + o, nc.sbuf_usable_end)

        A = ctx.enter_context(nc.psum_tensor("psum_a", [P, NT, 512], F32))
        B = ctx.enter_context(nc.psum_tensor("psum_b", [P, NT, 512], F32))
        M6 = ctx.enter_context(nc.psum_tensor("psum_m6", [P, 512], F32))
        M7 = ctx.enter_context(nc.psum_tensor("psum_m7", [P, 512], F32))
        AT, BT = A[:, :, 0:TW], B[:, :, 0:TW]
        AF = A[:, :, :].rearrange("p a b -> p (a b)")
        BFL = B[:, :, :].rearrange("p a b -> p (a b)")

        def tt(ap):
            return ap.rearrange("p (a b) -> p a b", a=NT)

        def col(i):
            return CUR[:, i:i + 1] if isinstance(i, int) else CUR[:, bass.ds(i, 1)]

        EPS_D, EPS_S, ONE = CST[:, 0:1], CST[:, 1:2], CST[:, 2:3]

        every = []

        def steps(name, names):
            s = Steps(ctx.enter_context(nc.semaphore(name)), names)
            every.append((name.rsplit("_", 1)[1], s))
            return s

        def ahead(eng, which):
            for owner, s in every:
                if owner == which:
                    eng.sem_inc(s.sem, 2 * len(s.names))

        def sem(name):
            return ctx.enter_context(nc.semaphore(name))

        rows_zero, rows_in, const_in = sem("rows_zero"), sem("rows_in"), sem("const_in")
        out_done = [sem("out0_done"), sem("out1_done")]
        start_dve, start_act, start_pe = sem("start_dve"), sem("start_act"), sem("start_pe")
        x_in = [sem("x_in0"), sem("x_in1")]
        x_pe, x_act, x_dve = sem("x_pe"), sem("x_act"), sem("x_dve")
        raw_in = [sem("raw0_in"), sem("raw1_in"), sem("bd_in")]
        w_ready, w_chain = sem("w_ready"), sem("w_chain")
        cur_ready = sem("cur_ready")
        past_pe, past_dve, past_po, past_act = sem("past_pe"), sem("past_dve"), sem("past_po"), sem("past_act")
        lru_pe = steps("lru_pe", ["x", "g", "r", "i"])
        lru_dve = steps("lru_dve", ["pad", "xev", "c2", "c1", "c0", "xcl", "gev", "ix", "d", "rd", "m2",
                                    "b", "scan", "y", "sq", "ss"])
        lru_act = steps("lru_act", ["c3", "xch", "gg", "r", "i", "t", "a", "m"])
        ln_pe = steps("lrunorm_pe", ["stat"])
        ln_act = steps("lrunorm_act", ["std"])
        ln_dve = steps("lrunorm_dve", ["zero", "rstd", "y0", "y1", "y2", "y3"])

        def rounds(i):
            r = [list(range(a, min(a + 4, i + 1))) for a in range(1, i + 1, 4)]
            return r + [[0]]

        h_pe = ["q", "k", "v", "vt0", "vt1", "vt2", "s0a", "s0b"]
        h_dve = ["qev", "qc", "qs0", "qs1", "qs2", "qs3", "qf", "ql0", "ql1",
                 "kev", "kc", "ks0", "ks1", "ks2", "ks3", "kf", "kl0", "kl1", "kl2", "kl3",
                 "vev", "vz", "vzl", "vl0", "vl1", "vl2"]
        h_act = ["qh0", "qh1", "kh0", "kh1", "kh2", "kh3", "vh0", "vh1", "vh2"]
        mxs = lambda i: [f"{x}{i}" for x in ("mx", "nb", "my", "nc")]
        exs = lambda i: [f"p{i}", f"q{i}"]
        h_dve += mxs(0)
        h_act += exs(0)
        for i in range(NQ):
            if i + 1 < NQ:
                h_pe += [f"s{i + 1}a", f"s{i + 1}b"]
                h_act += exs(i + 1)
            h_dve += [f"r{i}", f"u{i}", f"w{i}", f"x{i}"] + (["z0"] if i == 0 else [])
            if i + 1 < NQ:
                h_dve += mxs(i + 1)
            for r in range(len(rounds(i))):
                h_pe += [f"t{i}_{r}"]
                h_act += [f"th{i}_{r}"]
                h_dve += [f"tl{i}_{r}"]
            h_pe += [f"pv{i}"]
            h_act += [f"o{i}"]
        h_pe += ["stat"]
        h_act += ["sq", "std"]
        h_dve += ["rstd", "y"]
        hd_pe, hd_dve, hd_act = steps("head_pe", h_pe), steps("head_dve", h_dve), steps("head_act", h_act)

        ysp_act = steps("ysplit_act", [f"h{c}" for c in range(DC)])
        ysp_dve = steps("ysplit_dve", ["res", "zero"] + [f"l{c}" for c in range(DC)])
        wo_pe = steps("wout_pe", ["m0", "m1"])
        wo_act = steps("wout_act", ["y0", "sq0", "y1", "sq1"])
        wo_dve = steps("wout_dve", ["ss0", "ss1"])

        def boundary(name):
            d = ["rstd", "zero"]
            a = ["std"]
            dd, aa, pp = [], [], []
            for j in range(2):
                dd += ([f"res{j}"] if name == "f" else []) + [f"t{j}", f"hn{j}"]
                aa += [f"hh{j}", f"sq{j}"]
            dd += ["hl0", "ss0", "hl1", "ss1"]
            return (steps(name + "post_pe", ["stat"]), steps(name + "post_act", a), steps(name + "post_dve", d),
                    steps(name + "mix_dve", dd), steps(name + "mix_act", aa),
                    steps(name + "pre_pe", ["stat"]), steps(name + "pre_act", ["std"]),
                    steps(name + "pre_dve", ["rstd"]))

        Wb = boundary("w")
        Fb = boundary("f")
        up_pe = steps("up_pe", ["g0", "v0", "g1", "v1"])
        up_dve = steps("up_dve", [f"{x}{j}" for j in range(2) for x in ("pad", "ev", "c1", "c0", "gr", "f", "fl")])
        up_act = steps("up_act", [f"{x}{j}" for j in range(2) for x in ("c2", "ge", "fh")])
        dn_pe = steps("down_pe", [f"m{m}" for m in range(DC)])
        dn_dve = steps("down_dve", [f"a{m}" for m in range(DC)])
        ps_act = steps("postsq_act", [f"sq{m}" for m in range(DC)])
        ps_dve = steps("postsq_dve", ["zero"] + [f"ss{m}" for m in range(DC)])
        s0_pe, s0_act, s0_dve = steps("stat0_pe", ["stat"]), steps("stat0_act", ["std"]), steps("stat0_dve", ["rstd"])
        ep_pe, ep_act = sem("ep_pe"), sem("ep_act")

        block = ctx.enter_context(nc.Block())

        def tile(l, n):
            return l * TILES + n

        N_HEAD, N_WOUT, N_UP = 12, 24, 32
        W_CREDIT = 4

        def ready(n, l):
            return w_ready, l * TILES + n + (W_CREDIT + 1)

        @block.sync
        def _(sp):
            sp.wait_ge(rows_zero, 1)
            n = 0

            def rows(r0, src, count, tl=0):
                sp.dma_start(ROWS[r0:r0 + count, :, tl, :], src.rearrange("l (r p) -> r l p", p=P)).then_inc(rows_in, 16)

            rows(MIX_PRE, t["ln_mix_pre"], 8)
            rows(MIX_POST, t["ln_mix_post"], 8)
            rows(FFN_PRE, t["ln_ffn_pre"], 8)
            rows(FFN_POST, t["ln_ffn_post"], 8)
            rows(CONV_W, t["lru_conv_w"].rearrange("l k c -> l (k c)"), 16)
            rows(CONV_B, t["lru_conv_b"], 4)
            rows(GATE_BA, t["lru_ba"].rearrange("l n c -> l (n c)"), 4)
            rows(GATE_BX, t["lru_bx"].rearrange("l n c -> l (n c)"), 4)
            rows(A_PAR, t["lru_a_param"], 4)
            rows(OUT_NORM, t["lru_out_norm"], 4)
            rows(SUBLN, t["diff_subln"], 1)
            rows(0, t["ffn_conv_w"].rearrange("l k c -> l (k c)"), 72, 1)
            rows(72, t["ffn_conv_b"], 24, 1)
            for i, nm in enumerate(("lam_q1", "lam_q2", "lam_k1", "lam_k2")):
                sp.dma_start(ROWS[LAM + i:LAM + i + 1, :, 0, 0:DH],
                             t[nm].rearrange("l (r p) -> r l p", r=1)).then_inc(rows_in, 16)
            sp.dma_start(COS[:, :], t["cos"]).then_inc(const_in, 16)
            sp.dma_start(SIN[:, :], t["sin"]).then_inc(const_in, 16)
            sp.dma_start(XIN[0][0:META, :], t["meta_tokens"]).then_inc(x_in[0], 16)
            xt = t["x"][0].rearrange("(b p) d -> b p d", p=P)
            for b in range(8):
                if b >= 1:
                    sp.wait_ge(x_pe, b)
                sp.dma_start(XIN[(b + 1) % 2][:, :], xt[b]).then_inc(x_in[(b + 1) % 2], 16)

            def load(dst, src, r, l, n, back):
                sp.wait_ge(*ready(n - back, l))
                sp.dma_start(dst, src).then_inc(raw_in[r], 16)

            w_in = t["w_in"].rearrange("l (k p) n -> l p k n", p=P)
            w_out = t["w_out"].rearrange("l (k p) n -> l p k n", p=P)
            w_up = t["w_up"].rearrange("l (k p) n -> l p k n", p=P)
            w_dn = t["w_down"].rearrange("l (g p) (m n) -> l g p m n", p=P, n=P)

            def sl(w, l, c0):
                return w[bass.ds(l, 1), :, :, bass.ds(c0, P)].rearrange("a p k n -> p (a k) n")

            def dn(l, g):
                return w_dn[bass.ds(l, 1), bass.ds(g, 1)].rearrange("a b p m n -> p (a b m) n")

            sp.wait_ge(rows_zero, 2)
            with sp.Fori(0, L) as l:
                with sp.Fori(0, LRU_CH) as c:
                    load(RAW[0][:], sl(w_in, l, c * P), 0, l, c * 3, 2)
                    load(RAW[1][:], sl(w_in, l, c * P + 512), 1, l, c * 3 + 1, 2)
                    sp.wait_ge(*ready(c * 3 + 2 - 3, l))
                    for j, nm in enumerate(("lru_wa", "lru_wx")):
                        for e in range(2):
                            src = t[nm].rearrange("l (c e) a b -> l c e a b", e=2)
                            src = src[bass.ds(l, 1), bass.ds(c, 1), e].rearrange("x y a b -> a (x y) b")
                            sp.dma_start(BD[64 * e:64 * e + 64, j:j + 1, 64 * e:64 * e + 64], src).then_inc(raw_in[2], 16)
                with sp.Fori(0, HEADS) as h:
                    load(RAW[0][:], sl(w_in, l, h * P + 1024), 0, l, h * 3 + N_HEAD, 1)
                    load(RAW[1][:], sl(w_in, l, h * P + 1536), 1, l, h * 3 + (N_HEAD + 1), 3)
                    load(RAW[0][:], sl(w_in, l, h * P + 2048), 0, l, h * 3 + (N_HEAD + 2), 2)
                load(RAW[0][:], sl(w_out, l, 0), 0, l, N_WOUT, 1)
                load(RAW[1][:], sl(w_out, l, P), 1, l, N_WOUT + 1, 2)
                with sp.Fori(1, DC // 2) as m:
                    for j in range(2):
                        load(RAW[j][:], sl(w_out, l, m * 256 + P * j), j, l, m * 2 + (N_WOUT + j), 2)

                def up(g, n):
                    for j in range(G):
                        load(RAW[0][:], sl(w_up, l, g * 256 + P * j), 0, l, n + 2 * j, 2)
                        load(RAW[1][:], sl(w_up, l, g * 256 + (FF + P * j)), 1, l, n + (2 * j + 1), 2)

                def down(g, n):
                    for j in range(G):
                        load(RAW[j][:], dn(l, g * G + j), j, l, n + j, 2)

                up(0, N_UP)
                with sp.Fori(1, NG) as g:
                    up(g, g * 6 + (N_UP - 2))
                    down(g - 1, g * 6 + (N_UP + 2))
                down(NG - 1, N_UP + 6 * NG - 2)
            ot = out[0].rearrange("(b p) d -> b p d", p=P)
            for b in range(8):
                sp.wait_ge(ep_act, 2 * b + 2)
                sp.dma_start(ot[b], OUTB[b % 2][:, :]).then_inc(out_done[b % 2], 16)
            for e in range(2):
                sp.wait_ge(out_done[e], 16 * 4)

        @block.gpsimd
        def _(po):
            nc.gpsimd.memset(ROWS[:], 0.0).then_inc(rows_zero, 1)
            nc.gpsimd.memset(BD[:], 0.0).then_inc(w_ready, W_CREDIT)
            nc.gpsimd.memset(MASK[:], 0.0).then_inc(w_chain, 1)
            nc.gpsimd.memset(ONES[:], 1.0).then_inc(rows_zero, 1)
            nc.gpsimd.memset(IDENT[:], 0.0).then_inc(w_chain, 1)
            po.wait_ge(w_chain, 2)
            nc.gpsimd.memset(MASK[0:64, :], -1e30).then_inc(w_chain, 1)
            nc.gpsimd.affine_select(out=IDENT[:], in_=IDENT[:], compare_op=ALU.not_equal, fill=1.0, base=0,
                                    pattern=[[-1, P]], channel_multiplier=1).then_inc(w_chain, 1)
            C0 = 4
            CH = 2 * TILES

            def split(n, l, raw, hi, lo, gain):
                shape = [P, raw.shape[1], P]
                if gain is None:
                    g = ONE.rearrange("p (a b) -> p a b", a=1).to_broadcast(shape)
                else:
                    g = CUR[:, gain:gain + DC].rearrange("p (a b) -> p a b", b=1).to_broadcast(shape)
                nc.gpsimd.tensor_tensor(hi, raw, g, ALU.mult).then_inc(w_chain, 1)
                nc.gpsimd.tensor_tensor(raw, raw, g, ALU.mult).then_inc(w_chain, 1)
                po.wait_ge(w_chain, l * CH + n * 2 + (C0 + 2))
                nc.gpsimd.tensor_tensor(lo, raw, hi.bitcast(F32), ALU.subtract).then_inc(w_ready, 1)

            def piece(n, l, r, count, slot, gain):
                per = [52, 48, 4][r]
                step = 64 if r == 2 else 16
                po.wait_ge(raw_in[r], l * (per * step) + count * step + step)
                if r == 2:
                    split(n, l, BD[:], BDH[:], BDL[:], gain)
                else:
                    split(n, l, RAW[r][:], WH[slot][:], WL[slot][:], gain)

            po.wait_ge(start_dve, 1)
            with po.Fori(0, L) as l:
                po.wait_ge(cur_ready, l + 1)
                po.wait_ge(*up_pe.at("v1", l * NG - 1))
                po.wait_ge(*dn_pe.at("m7", l * NG - 1))
                po.sem_inc(past_po, 1)
                with po.Fori(0, LRU_CH) as c:
                    k = l * LRU_CH + c
                    po.wait_ge(*lru_pe.at("x", k - 1))
                    piece(c * 3, l, 0, c, 0, MIX_PRE)
                    po.wait_ge(*lru_pe.at("g", k - 1))
                    piece(c * 3 + 1, l, 1, c, 1, MIX_PRE)
                    po.wait_ge(*lru_pe.at("i", k - 1))
                    piece(c * 3 + 2, l, 2, c, 2, None)
                po.wait_ge(*lru_pe.at("g", l * LRU_CH + 3))
                po.sem_inc(past_po, 1)
                with po.Fori(0, HEADS) as h:
                    k = l * HEADS + h
                    po.wait_ge(*hd_pe.at("v", k - 1))
                    piece(h * 3 + N_HEAD, l, 0, h * 2 + 4, 0, MIX_PRE)
                    po.wait_ge(*hd_pe.at("k", k - 1))
                    piece(h * 3 + (N_HEAD + 1), l, 1, h + 4, 1, MIX_PRE)
                    po.wait_ge(*hd_pe.at("q", k))
                    piece(h * 3 + (N_HEAD + 2), l, 0, h * 2 + 5, 0, MIX_PRE)
                po.wait_ge(*hd_pe.at("v", l * HEADS + 3))
                po.sem_inc(past_po, 1)
                with po.Fori(0, DC // 2) as m:
                    for j in range(2):
                        po.wait_ge(*wo_pe.at(f"m{j}", l * 4 + m - 1))
                        piece(m * 2 + (N_WOUT + j), l, j, m + (12 if j == 0 else 8), j, None)

                def up(g, n, c0, c1, prev):
                    for j in range(G):
                        for e, nm in enumerate(("g", "v")):
                            if prev is not None and j == 0:
                                po.wait_ge(*up_pe.at(f"{nm}1", prev))
                            if j == 1:
                                po.wait_ge(*up_pe.at(f"{nm}0", l * NG + g))
                            piece(n + (2 * j + e), l, e, (c0, c1)[e] + j, e, FFN_PRE)

                def down(g, n, c0, c1):
                    po.wait_ge(*dn_pe.at("m7", l * NG + g - 1))
                    for j in range(G):
                        piece(n + j, l, j, (c0, c1)[j], 2 + j, None)

                po.wait_ge(*wo_pe.at("m1", l * 4 + 3))
                up(0, N_UP, 16, 12, None)
                with po.Fori(1, NG) as g:
                    up(g, g * 6 + (N_UP - 2), g * 3 + 15, g * 3 + 11, l * NG + g - 1)
                    down(g - 1, g * 6 + (N_UP + 2), g * 3 + 17, g * 3 + 13)
                down(NG - 1, N_UP + 6 * NG - 2, 16 + 35, 12 + 35)

        @block.tensor
        def _(pe):
            def product(ps, wh, wl, xh, xl, tiles=range(NT)):
                n = wh.shape[1]
                for t_ in tiles:
                    for c in range(n):
                        pe.matmul(ps[:, t_, 0:TW], wh[:, c, :], xh(c, t_), start=(c == 0), stop=False)
                        pe.matmul(ps[:, t_, 0:TW], wh[:, c, :], xl(c, t_), start=False, stop=False)
                        m = pe.matmul(ps[:, t_, 0:TW], wl[:, c, :], xh(c, t_), start=False, stop=(c == n - 1))
                return m

            def hs(w):
                return (lambda c, t_: HH[:, c, TW * t_:TW * t_ + TW]), (lambda c, t_: HL[:, c, TW * t_:TW * t_ + TW])

            def project(ps, slot):
                return product(ps, WH[slot], WL[slot], *hs(slot))

            def stat(ps, src):
                for t_ in range(NT):
                    m = pe.matmul(ps[:, t_, 0:TW], ONES[:, :], src[:, TW * t_:TW * t_ + TW], start=True, stop=True)
                return m

            ahead(pe, "pe")
            pe.wait_ge(w_chain, 4)
            pe.wait_ge(rows_in, 16 * 17)
            for l in range(L):
                for e in range(2):
                    m = pe.transpose(M6[:, (2 * l + e) * P:(2 * l + e + 1) * P], ROWS[:, l, e, :], IDENT[:, :])
            m.then_inc(start_pe, 1)
            pe.wait_ge(rows_zero, 2)
            pe.wait_ge(start_dve, 3)
            pe.matmul(M7[:, 0:2 * L], ONES[:, :], SM[:, 0:2 * L], start=True, stop=True).then_inc(start_pe, 1)
            for b in range(9):
                rows, buf = (META, 0) if b == 0 else (P, b % 2)
                ps = (A, B)[b % 2]
                pe.wait_ge(x_in[buf], 16 * (b // 2 + 1))
                if b >= 2:
                    pe.wait_ge(x_act, 2 * b - 2)
                for c in range(DC):
                    m = pe.transpose(ps[:, c // 4, (c % 4) * P:(c % 4) * P + rows],
                                     XIN[buf][0:rows, c * P:(c + 1) * P], IDENT[0:rows, 0:rows])
                m.then_inc(x_pe, 1)
            pe.wait_ge(x_dve, 18)
            stat(A, S[3]).then_inc(*s0_pe.inc("stat"))

            with pe.Fori(0, L) as l:
                pe.wait_ge(*Fb[7].at("rstd", l - 1))
                pe.wait_ge(*s0_dve.at("rstd", 0))
                pe.sem_inc(past_pe, 1)
                with pe.Fori(0, LRU_CH) as c:
                    k = l * LRU_CH + c
                    pe.wait_ge(*ready(c * 3, l))
                    pe.wait_ge(*lru_act.at("r", k - 1))
                    project(A, 0).then_inc(*lru_pe.inc("x"))
                    pe.wait_ge(*ready(c * 3 + 1, l))
                    pe.wait_ge(*lru_act.at("i", k - 1))
                    project(B, 1).then_inc(*lru_pe.inc("g"))
                    pe.wait_ge(*ready(c * 3 + 2, l))
                    pe.wait_ge(*lru_dve.at("xcl", k))
                    xs = (lambda c_, t_: XH[:, TW * t_:TW * t_ + TW]), (lambda c_, t_: XL[:, TW * t_:TW * t_ + TW])
                    product(A, BDH[:, 0:1, :], BDL[:, 0:1, :], *xs).then_inc(*lru_pe.inc("r"))
                    pe.wait_ge(*lru_dve.at("gev", k))
                    product(B, BDH[:, 1:2, :], BDL[:, 1:2, :], *xs).then_inc(*lru_pe.inc("i"))
                pe.wait_ge(*lru_act.at("i", l * 4 + 3))
                pe.wait_ge(*lru_dve.at("ss", l * 4 + 3))
                stat(A, S[2]).then_inc(*ln_pe.inc("stat"))
                pe.wait_ge(*ln_act.at("std", l))
                pe.matmul(M7[:, 0:2], ONES[:, :], ONES[:, 0:2], start=True, stop=True)
                with pe.Fori(0, HEADS) as h:
                    k = l * HEADS + h
                    pe.wait_ge(*ready(h * 3 + N_HEAD, l))
                    pe.wait_ge(*hd_act.at("std", k - 1))
                    project(A, 0).then_inc(*hd_pe.inc("q"))
                    pe.wait_ge(*ready(h * 3 + (N_HEAD + 1), l))
                    pe.wait_ge(*hd_act.at("q8", k - 1))
                    project(B, 1).then_inc(*hd_pe.inc("k"))
                    pe.wait_ge(*ready(h * 3 + (N_HEAD + 2), l))
                    pe.wait_ge(*hd_dve.at("qev", k))
                    project(A, 0).then_inc(*hd_pe.inc("v"))
                    pe.wait_ge(*hd_dve.at("vev", k))
                    for r, (ps, blocks) in enumerate(((M6, [1, 2, 3, 4]), (M7, [5, 6, 7, 8]), (M6, [0]))):
                        if r == 2:
                            pe.wait_ge(*hd_dve.at("vl0", k))
                        for n, b in enumerate(blocks):
                            t0 = META + P * (b - 1) if b else 0
                            m = pe.transpose(ps[:, n * P:(n + 1) * P], S[0][:, t0:t0 + P], IDENT[:, :])
                        m.then_inc(*hd_pe.inc(f"vt{r}"))

                    def scores(i):
                        q0, keys = (0, META) if i == 0 else (META + P * (i - 1), META + P * i)
                        if i == 0:
                            pe.wait_ge(*hd_dve.at("kl3", k))
                            pe.wait_ge(*hd_dve.at("vev", k))
                        for mp, ps in ((0, AF), (1, BFL)):
                            if i >= 1:
                                pe.wait_ge(*hd_act.at(f"{'pq'[mp]}{i - 1}", k))
                            for b0 in range(0, keys, 512):
                                b1 = min(b0 + 512, keys)
                                m0 = max(b0, keys - 64)
                                masked = i >= 1 and m0 < b1
                                pe.matmul(ps[:, b0:b1], QS[:, mp, q0:q0 + P], KH[:, mp, b0:b1], start=True, stop=False)
                                m = pe.matmul(ps[:, b0:b1], QS[:, mp, q0:q0 + P], KL[:, mp, b0:b1],
                                              start=False, stop=not masked)
                                if masked:
                                    m = pe.matmul(ps[:, m0:b1], IDENT[:, :], MASK[:, 0:b1 - m0], start=False, stop=True)
                            m.then_inc(*hd_pe.inc(f"s{i}{'ab'[mp]}"))

                    scores(0)
                    for i in range(NQ):
                        if i + 1 < NQ:
                            scores(i + 1)
                        w = S[2 * (i % 2)]
                        pe.wait_ge(*hd_dve.at(f"x{i}", k))
                        if i == 0:
                            pe.wait_ge(*hd_dve.at("z0", k))
                        for r, blocks in enumerate(rounds(i)):
                            if r >= 1:
                                pe.wait_ge(*hd_dve.at(f"tl{i}_{r - 1}", k))
                            elif i >= 1:
                                pe.wait_ge(*hd_dve.at(f"tl{i - 1}_{len(rounds(i - 1)) - 1}", k))
                            else:
                                pe.wait_ge(*hd_dve.at("vl2", k))
                            for n, b in enumerate(blocks):
                                t0 = META + P * (b - 1) if b else 0
                                m = pe.transpose(M6[:, n * P:(n + 1) * P], w[:, t0:t0 + P], IDENT[:, :])
                            m.then_inc(*hd_pe.inc(f"t{i}_{r}"))
                        pe.wait_ge(*hd_dve.at(f"tl{i}_{len(rounds(i)) - 1}", k))
                        if i >= 1:
                            pe.wait_ge(*hd_act.at(f"o{i - 1}", k))
                        for b in range(i + 1):
                            ph = PTH[:, b, :]
                            pe.matmul(M7[:, 0:P], VH[:, b, :], ph, start=(b == 0), stop=False)
                            pe.matmul(M7[:, 0:P], VH[:, b, :], PTL[:, b, :], start=False, stop=False)
                            m = pe.matmul(M7[:, 0:P], VL[:, b, :], ph, start=False, stop=(b == i))
                        m.then_inc(*hd_pe.inc(f"pv{i}"))
                    pe.wait_ge(*hd_act.at("sq", k))
                    stat(A, S[0]).then_inc(*hd_pe.inc("stat"))
                pe.wait_ge(*ysp_dve.at("l7", l))
                pe.wait_ge(*hd_act.at("std", l * 4 + 3))
                pe.matmul(M7[:, 0:2], ONES[:, :], ONES[:, 0:2], start=True, stop=True)
                with pe.Fori(0, DC // 2) as m_:
                    for j, ps in enumerate((A, B)):
                        pe.wait_ge(*ready(m_ * 2 + (N_WOUT + j), l))
                        pe.wait_ge(*wo_act.at(f"sq{j}", l * 4 + m_ - 1))
                        project(ps, j).then_inc(*wo_pe.inc(f"m{j}"))
                pe.wait_ge(*wo_dve.at("ss1", l * 4 + 3))
                stat(A, S[2]).then_inc(*Wb[0].inc("stat"))
                pe.wait_ge(*Wb[3].at("ss1", l * 4 + 3))
                stat(A, S[2]).then_inc(*Wb[5].inc("stat"))
                pe.wait_ge(*Wb[6].at("std", l))

                def up(g, n, prev):
                    for j in range(G):
                        for e, ps in enumerate((A, B)):
                            pe.wait_ge(*ready(n + (2 * j + e), l))
                            kk = l * NG + g
                            if j == 1:
                                pe.wait_ge(*up_dve.at(("ev0", "f0")[e], kk))
                            elif prev == "up":
                                pe.wait_ge(*up_dve.at(("ev1", "f1")[e], kk - 1))
                            elif prev == "down":
                                pe.wait_ge(*dn_dve.at(("a6", "a7")[e], kk - 2))
                            project(ps, e).then_inc(*up_pe.inc(f"{'gv'[e]}{j}"))

                def down(g, n, fs, final=False):
                    kk = l * NG + g
                    pe.wait_ge(*ready(n + 1, l))
                    pe.wait_ge(*up_dve.at("fl1", kk))
                    for m in range(DC):
                        ps = (A, B)[m % 2]
                        if m < 2 and not final:
                            pe.wait_ge(*up_dve.at(("ev1", "f1")[m], kk + 1))
                        elif m >= 2:
                            pe.wait_ge(*dn_dve.at(f"a{m - 2}", kk))
                        else:
                            pe.wait_ge(*dn_dve.at(f"a{m + 6}", kk - 1))
                        for t_ in range(NT):
                            for j in range(G):
                                fh = FH[:, fs + j, TW * t_:TW * t_ + TW]
                                fl = FL[:, fs + j, TW * t_:TW * t_ + TW]
                                q = pe.matmul(ps[:, t_, 0:TW], WH[2 + j][:, m, :], fh, start=(j == 0), stop=False)
                                q = pe.matmul(ps[:, t_, 0:TW], WH[2 + j][:, m, :], fl, start=False, stop=False)
                                q = pe.matmul(ps[:, t_, 0:TW], WL[2 + j][:, m, :], fh, start=False, stop=(j == G - 1))
                        q.then_inc(*dn_pe.inc(f"m{m}"))

                last = NG - 1
                up(0, N_UP, "")
                up(1, N_UP + 4, "up")
                down(0, N_UP + 8, 0)
                with pe.Fori(1, NG // 2) as g2:
                    g = g2 * 2
                    up(g, g * 6 + (N_UP - 2), "down")
                    down(g - 1, g * 6 + (N_UP + 2), 2)
                    up(g + 1, g * 6 + (N_UP + 4), "down")
                    down(g, g * 6 + (N_UP + 8), 0)
                down(last, N_UP + 6 * NG - 2, 2, final=True)
                pe.wait_ge(*ps_dve.at("ss7", l))
                pe.wait_ge(*dn_dve.at("a7", l * NG + last))
                stat(A, Lb[4]).then_inc(*Fb[0].inc("stat"))
                pe.wait_ge(*Fb[3].at("ss1", l * 4 + 3))
                stat(A, Lb[4]).then_inc(*Fb[5].inc("stat"))
            pe.wait_ge(*Fb[7].at("rstd", L - 1))
            for b in range(8):
                ps = (A, B)[b % 2]
                if b >= 2:
                    pe.wait_ge(ep_act, 2 * b - 2)
                for c in range(DC):
                    t0 = META + P * b
                    m = pe.transpose(ps[:, c // 4, (c % 4) * P:(c % 4 + 1) * P], ACC[:, c, t0:t0 + P], IDENT[:, :])
                m.then_inc(ep_pe, 1)

        @block.scalar
        def _(ac):
            def act(dst, src, f, **kw):
                return nc.scalar.activation(dst, src, f, **kw)

            def std(dst, ps, width, eps):
                return act(tt(dst[:, 0:T]), ps[:, :, 0:TW], ACT.Sqrt, scale=1.0 / width, bias=eps)

            ahead(ac, "act")
            ac.wait_ge(start_dve, 4)
            ac.wait_ge(start_pe, 2)
            act(SM[:, 8:8 + 2 * L], M7[:, 0:2 * L], ACT.Exp).then_inc(start_act, 1)
            ac.wait_ge(start_dve, 6)
            act(SM[:, 24:32], SM[:, 16:24], ACT.Exp, scale=-1.0).then_inc(start_act, 1)
            for b in range(9):
                rows, ps = (META if b == 0 else P), (A, B)[b % 2]
                t0 = 0 if b == 0 else META + P * (b - 1)
                src = ps[:, 0:2, :].rearrange("p a b -> p (a b)").rearrange("p (c t) -> p c t", t=P)[:, :, 0:rows]
                ac.wait_ge(x_pe, b + 1)
                act(HH[:, :, t0:t0 + rows], src, ACT.Copy).then_inc(x_act, 1)
                if b >= 1:
                    ac.wait_ge(x_dve, 2 * b)
                ac.wait_ge(x_dve, 2 * b + 1)
                act(SQ8[:, :, 0:rows], src, ACT.Square).then_inc(x_act, 1)
            ac.wait_ge(*s0_pe.at("stat", 0))
            std(RSTD, A, D, EPS_D).then_inc(*s0_act.inc("std"))

            with ac.Fori(0, L) as l:
                with ac.Fori(0, LRU_CH) as c:
                    k = l * LRU_CH + c
                    ac.wait_ge(*lru_dve.at("xev", k))
                    act(XC[:, :], XPAD[:, 3:3 + T], ACT.Identity, scale=col(c + (CONV_W + 12)),
                        bias=col(c + CONV_B)).then_inc(*lru_act.inc("c3"))
                    ac.wait_ge(*lru_dve.at("c0", k))
                    act(XH[:, :], XC[:, :], ACT.Copy).then_inc(*lru_act.inc("xch"))
                    ac.wait_ge(*lru_dve.at("gev", k))
                    act(GG[:, :], GG[:, :], ACT.Gelu_apprx_tanh).then_inc(*lru_act.inc("gg"))
                    ac.wait_ge(*lru_pe.at("r", k))
                    act(tt(RA[:, :]), AT, ACT.Sigmoid, bias=col(c + GATE_BA)).then_inc(*lru_act.inc("r"))
                    ac.wait_ge(*lru_pe.at("i", k))
                    act(tt(IB[:, :]), BT, ACT.Sigmoid, bias=col(c + GATE_BX)).then_inc(*lru_act.inc("i"))
                    ac.wait_ge(*lru_act.at("r", k))
                    ac.wait_ge(*lru_dve.at("ss", k - 1))
                    act(S[1][:, 0:T], RA[:, :], ACT.Tanh, scale=col(c + NEG_C)).then_inc(*lru_act.inc("t"))
                    ac.wait_ge(*lru_act.at("t", k))
                    act(RA[:, :], RA[:, :], ACT.Exp, scale=col(c + POS_C)).then_inc(*lru_act.inc("a"))
                    ac.wait_ge(*lru_dve.at("m2", k))
                    act(S[0][:, 0:T], S[0][:, 0:T], ACT.Sqrt).then_inc(*lru_act.inc("m"))
                ac.wait_ge(*ln_pe.at("stat", l))
                std(S[3], A, 512, EPS_D).then_inc(*ln_act.inc("std"))
                with ac.Fori(0, HEADS) as h:
                    k = l * HEADS + h
                    ac.wait_ge(*hd_dve.at("qf", k))
                    act(QS[0:64, 0, :], S[0][0:64, 0:T], ACT.Copy).then_inc(*hd_act.inc("qh0"))
                    act(QS[64:128, 1, :], S[0][64:128, 0:T], ACT.Copy).then_inc(*hd_act.inc("qh1"))
                    ac.wait_ge(*hd_dve.at("kf", k))
                    act(KH[0:64, 0, :], S[0][0:64, 0:T], ACT.Copy).then_inc(*hd_act.inc("kh0"))
                    act(KH[64:128, 0, :], S[0][0:64, 0:T], ACT.Copy).then_inc(*hd_act.inc("kh1"))
                    act(KH[64:128, 1, :], S[0][64:128, 0:T], ACT.Copy).then_inc(*hd_act.inc("kh2"))
                    act(KH[0:64, 1, :], S[0][64:128, 0:T], ACT.Copy).then_inc(*hd_act.inc("kh3"))
                    for r, (ps, b0, nb) in enumerate(((M6, 1, 4), (M7, 5, 4), (M6, 0, 1))):
                        ac.wait_ge(*hd_pe.at(f"vt{r}", k))
                        if r == 2:
                            ac.wait_ge(*hd_dve.at("vzl", k))
                        rows = META if r == 2 else P
                        act(VH[0:rows, b0:b0 + nb, :], ps[0:rows, 0:nb * P].rearrange("p (a b) -> p a b", b=P),
                            ACT.Copy).then_inc(*hd_act.inc(f"vh{r}"))

                    def exps(i):
                        keys = META + P * i
                        for mp, ps in ((0, AF), (1, BFL)):
                            dst = S[2 * (i % 2) + mp]
                            ac.wait_ge(*hd_dve.at(f"{('nb', 'nc')[mp]}{i}", k))
                            if i == 0:
                                ac.wait_ge(*hd_dve.at("vl2", k))
                            if i >= 2:
                                ac.wait_ge(*hd_pe.at(f"t{i - 2}_{len(rounds(i - 2)) - 1}", k))
                            act(dst[:, 0:keys], ps[:, 0:keys], ACT.Exp, scale=DH ** -0.5, bias=SM[:, 34 + mp:35 + mp],
                                accum_out=SM[:, 36 + mp + 2 * (i % 2):37 + mp + 2 * (i % 2)]
                                ).then_inc(*hd_act.inc(f"{'pq'[mp]}{i}"))

                    exps(0)
                    for i in range(NQ):
                        if i + 1 < NQ:
                            exps(i + 1)
                        for r, blocks in enumerate(rounds(i)):
                            ac.wait_ge(*hd_pe.at(f"t{i}_{r}", k))
                            if i >= 1 and r == 0:
                                ac.wait_ge(*hd_pe.at(f"pv{i - 1}", k))
                            b0, nb = blocks[0], len(blocks)
                            act(PTH[:, b0:b0 + nb, :], M6[:, 0:nb * P].rearrange("p (a b) -> p a b", b=P),
                                ACT.Copy).then_inc(*hd_act.inc(f"th{i}_{r}"))
                        ac.wait_ge(*hd_pe.at(f"pv{i}", k))
                        q0, qn = (0, META) if i == 0 else (META + P * (i - 1), P)
                        act(ACC[:, bass.ds(h + 4, 1), q0:q0 + qn].rearrange("p a b -> p (a b)"), M7[:, 0:qn],
                            ACT.Copy).then_inc(*hd_act.inc(f"o{i}"))
                    ac.wait_ge(*hd_act.at("o8", k))
                    ac.sem_inc(past_act, 1)
                    act(S[0][:, 0:T], ACC[:, bass.ds(h + 4, 1), :].rearrange("p a b -> p (a b)"),
                        ACT.Square).then_inc(*hd_act.inc("sq"))
                    ac.wait_ge(*hd_pe.at("stat", k))
                    std(S[1], A, P, EPS_S).then_inc(*hd_act.inc("std"))
                for c in range(DC):
                    ac.wait_ge(*ysp_dve.at("res", l))
                    act(HH[:, c, :], ACC[:, c, :], ACT.Copy).then_inc(*ysp_act.inc(f"h{c}"))
                with ac.Fori(0, DC // 2) as m:
                    for j, ps in enumerate((AT, BT)):
                        kk = l * 4 + m
                        ac.wait_ge(*wo_pe.at(f"m{j}", kk))
                        act(ACC[:, bass.ds(m * 2 + j, 1), :].rearrange("p x (a b) -> p (x a) b", a=NT), ps,
                            ACT.Copy).then_inc(*wo_act.inc(f"y{j}"))
                        ac.wait_ge(*wo_dve.at(f"ss{j}", kk - 1))
                        act(tt(S[j][:, 0:T]), ps, ACT.Square).then_inc(*wo_act.inc(f"sq{j}"))

                def mix(Bd, r2):
                    ac.wait_ge(*Bd[0].at("stat", l))
                    std(r2, A, D, EPS_D).then_inc(*Bd[1].inc("std"))
                    with ac.Fori(0, 4) as c2:
                        kk = l * 4 + c2
                        for j in range(2):
                            cc = bass.ds(c2 * 2 + j, 1)
                            new = ACC[:, cc, :].rearrange("p a b -> p (a b)")
                            ac.wait_ge(*Bd[3].at(f"hn{j}", kk))
                            ac.sem_inc(past_act, 1)
                            act(HH[:, cc, :].rearrange("p a b -> p (a b)"), new, ACT.Copy).then_inc(*Bd[4].inc(f"hh{j}"))
                            ac.wait_ge(*Bd[3].at(f"ss{j}", kk - 1))
                            ac.sem_inc(past_act, 1)
                            act(S[j][:, 0:T], new, ACT.Square).then_inc(*Bd[4].inc(f"sq{j}"))
                    ac.wait_ge(*Bd[5].at("stat", l))
                    std(RSTD, A, D, EPS_D).then_inc(*Bd[6].inc("std"))

                mix(Wb, S[3])

                def gate(g, fs):
                    kk = l * NG + g
                    for j in range(G):
                        ac.wait_ge(*up_dve.at(f"ev{j}", kk))
                        act(S[1][:, 0:T], S[0][:, 2:2 + T], ACT.Identity, scale=col(g * 2 + (FCONV_W + 48 + j)),
                            bias=col(g * 2 + (FCONV_B + j))).then_inc(*up_act.inc(f"c2{j}"))
                        ac.wait_ge(*up_dve.at(f"c0{j}", kk))
                        act(S[2][:, 0:T], S[1][:, 0:T], ACT.Gelu_apprx_tanh).then_inc(*up_act.inc(f"ge{j}"))
                        ac.wait_ge(*up_dve.at(f"f{j}", kk))
                        ac.wait_ge(*dn_pe.at("m7", kk - 2))
                        act(FH[:, fs + j, :], S[3][:, 0:T], ACT.Copy).then_inc(*up_act.inc(f"fh{j}"))

                with ac.Fori(0, NG // 2) as g2:
                    gate(g2 * 2, 0)
                    gate(g2 * 2 + 1, 2)
                for m in range(DC):
                    ac.wait_ge(*dn_dve.at(f"a{m}", l * NG + NG - 1))
                    if m >= 2:
                        ac.wait_ge(*ps_dve.at(f"ss{m - 2}", l))
                    act(Lb[m % 2][:, :], ACC[:, m, :], ACT.Square).then_inc(*ps_act.inc(f"sq{m}"))
                mix(Fb, Lb[5])
            for b in range(8):
                ac.wait_ge(ep_pe, b + 1)
                if b >= 2:
                    ac.wait_ge(out_done[b % 2], 16 * (b // 2))
                for e in range(2):
                    act(OUTB[b % 2][:, 512 * e:512 * e + 512], (A, B)[b % 2][:, e, :], ACT.Copy).then_inc(ep_act, 1)

        @block.vector
        def _(dv):
            v = nc.vector
            ahead(dv, "dve")

            def flat(ap):
                return ap.rearrange("p a b -> p (a b)")

            v.memset(CST[:, 0:1], 1e-6)
            v.memset(CST[:, 1:2], 1e-5)
            v.memset(CST[:, 3:6], 0.0)
            v.memset(CST[:, 2:3], 1.0).then_inc(start_dve, 1)
            v.memset(HH[:, :, TOK:T].bitcast(F32), 0.0)
            v.memset(HL[:, :, TOK:T].bitcast(F32), 0.0)
            v.memset(S[3][:, TOK:T], 0.0)
            v.memset(ACC[:, :, TOK:T], 0.0)
            dv.wait_ge(start_pe, 1)
            v.tensor_copy(PAR[:, :, :], M6[:, :].rearrange("p (l n) -> p l n", l=L)).then_inc(start_dve, 1)
            dv.wait_ge(start_dve, 2)
            v.tensor_tensor(SM[:, 0:2 * L].rearrange("p (l n) -> p l n", l=L), PAR[:, :, LAM:LAM + 2],
                            PAR[:, :, LAM + 2:LAM + 4], ALU.mult).then_inc(start_dve, 1)
            v.tensor_scalar(SM[:, 16:24].rearrange("p (l n) -> p l n", l=L), PAR[:, :, A_PAR:A_PAR + 4], -1.0, None,
                            ALU.mult).then_inc(start_dve, 1)
            dv.wait_ge(start_dve, 4)
            am = SM[:, 32:40]
            v.tensor_scalar(am.rearrange("p (l n) -> p l n", l=L), PAR[:, :, A_PAR:A_PAR + 4], 0.0, None,
                            ALU.min).then_inc(start_dve, 1)
            v.tensor_tensor(SM[:, 16:24].rearrange("p (l n) -> p l n", l=L), PAR[:, :, A_PAR:A_PAR + 4],
                            SM[:, 16:24].rearrange("p (l n) -> p l n", l=L), ALU.max).then_inc(start_dve, 1)
            n = [6]

            def link(ins):
                n[0] += 1
                ins.then_inc(start_dve, 1)
                dv.wait_ge(start_dve, n[0])

            dv.wait_ge(start_act, 2)
            e, w, w2, p = SM[:, 24:32], SM[:, 40:48], SM[:, 48:56], SM[:, 56:64]
            link(v.tensor_scalar(w, e, 2.0, None, ALU.add))
            link(v.reciprocal(w, w))
            link(v.tensor_tensor(w, w, e, ALU.mult))
            link(v.tensor_tensor(w2, w, w, ALU.mult))
            link(v.tensor_scalar(p, w2, 1.0 / 19, 1.0 / 17, ALU.mult, ALU.add))
            for q in (15, 13, 11, 9, 7, 5, 3, 1):
                link(v.tensor_tensor(p, p, w2, ALU.mult))
                link(v.tensor_scalar(p, p, 1.0 / q, None, ALU.add))
            link(v.tensor_tensor(p, p, w, ALU.mult))
            link(v.scalar_tensor_tensor(out=p, in0=p, scalar=-2.0, in1=am, op0=ALU.mult, op1=ALU.add))
            pl = p.rearrange("p (l n) -> p l n", l=L)
            link(v.tensor_scalar(PAR[:, :, POS_C:POS_C + 4], pl, 8.0, None, ALU.mult))
            link(v.tensor_scalar(PAR[:, :, NEG_C:NEG_C + 4], pl, -8.0, None, ALU.mult))
            for l in range(L):
                li = LAMBDA_INIT[l]
                link(v.tensor_tensor(PAR[:, l, NEG_LAM:NEG_LAM + 1], SM[:, 9 + 2 * l:10 + 2 * l],
                                     SM[:, 8 + 2 * l:9 + 2 * l], ALU.subtract))
                link(v.tensor_scalar(PAR[:, l, NEG_LAM:NEG_LAM + 1], PAR[:, l, NEG_LAM:NEG_LAM + 1], -li, None, ALU.add))
                link(v.tensor_scalar(PAR[:, l, HEAD_GAIN:HEAD_GAIN + 1], PAR[:, l, SUBLN:SUBLN + 1], 1.0 - li, None,
                                     ALU.mult))
            for b in range(9):
                rows, ps = (META if b == 0 else P), (A, B)[b % 2]
                t0 = 0 if b == 0 else META + P * (b - 1)
                src = ps[:, 0:2, :].rearrange("p a b -> p (a b)").rearrange("p (c t) -> p c t", t=P)[:, :, 0:rows]
                dv.wait_ge(x_act, 2 * b + 1)
                v.tensor_tensor(HL[:, :, t0:t0 + rows], src, HH[:, :, t0:t0 + rows].bitcast(F32),
                                ALU.subtract).then_inc(x_dve, 1)
                dv.wait_ge(x_act, 2 * b + 2)
                v.tensor_reduce(S[3][:, t0:t0 + rows], SQ8[:, :, 0:rows].rearrange("p c t -> p t c"), AX_X,
                                ALU.add).then_inc(x_dve, 1)
            dv.wait_ge(const_in, 32)
            dv.wait_ge(*s0_act.at("std", 0))
            v.reciprocal(RSTD[:, 0:T], RSTD[:, 0:T]).then_inc(*s0_dve.inc("rstd"))

            R = RSTD[:, 0:T]
            with dv.Fori(0, L) as l:
                dv.wait_ge(*Fb[7].at("rstd", l - 1))
                v.tensor_copy(CUR[:, :], flat(PAR[:, bass.ds(l, 1), :])).then_inc(cur_ready, 1)
                v.memset(S[2][:, 0:T], 0.0).then_inc(*ln_dve.inc("zero"))
                dv.wait_ge(cur_ready, l + 1)
                dv.wait_ge(*s0_dve.at("rstd", 0))
                dv.wait_ge(*ln_dve.at("zero", l))
                dv.sem_inc(past_dve, 1)
                with dv.Fori(0, LRU_CH) as c:
                    k = l * LRU_CH + c
                    D_ = lambda nm: dv.wait_ge(*lru_dve.at(nm, k))
                    v.memset(XPAD[:, 0:3], 0.0).then_inc(*lru_dve.inc("pad"))
                    dv.wait_ge(*lru_pe.at("x", k))
                    v.tensor_tensor(tt(XPAD[:, 3:3 + T]), AT, tt(R), ALU.mult).then_inc(*lru_dve.inc("xev"))
                    dv.wait_ge(*lru_act.at("c3", k))
                    for j, nm in ((2, "c2"), (1, "c1"), (0, "c0")):
                        D_({2: "xev", 1: "c2", 0: "c1"}[j])
                        v.scalar_tensor_tensor(out=XC[:, :], in0=XPAD[:, j:j + T], scalar=col(c + (CONV_W + 4 * j)),
                                               in1=XC[:, :], op0=ALU.mult, op1=ALU.add).then_inc(*lru_dve.inc(nm))
                    dv.wait_ge(*lru_act.at("xch", k))
                    v.tensor_tensor(XL[:, :], XC[:, :], XH[:, :].bitcast(F32), ALU.subtract).then_inc(*lru_dve.inc("xcl"))
                    dv.wait_ge(*lru_pe.at("g", k))
                    v.tensor_tensor(tt(GG[:, :]), BT, tt(R), ALU.mult).then_inc(*lru_dve.inc("gev"))
                    dv.wait_ge(*lru_act.at("i", k))
                    v.tensor_tensor(IB[:, :], IB[:, :], XC[:, :], ALU.mult).then_inc(*lru_dve.inc("ix"))
                    dv.wait_ge(*lru_act.at("t", k))
                    s0, s1 = S[0][:, 0:T], S[1][:, 0:T]
                    v.tensor_scalar(s0, s1, 1.0, None, ALU.add).then_inc(*lru_dve.inc("d"))
                    D_("d")
                    v.reciprocal(s0, s0).then_inc(*lru_dve.inc("rd"))
                    D_("rd")
                    v.scalar_tensor_tensor(out=s0, in0=s1, scalar=2.0, in1=s0, op0=ALU.mult,
                                           op1=ALU.mult).then_inc(*lru_dve.inc("m2"))
                    dv.wait_ge(*lru_act.at("m", k))
                    D_("ix")
                    v.tensor_tensor(IB[:, :], IB[:, :], s0, ALU.mult).then_inc(*lru_dve.inc("b"))
                    D_("b")
                    v.tensor_tensor_scan(s1, RA[:, :], IB[:, :], 0.0, ALU.mult, ALU.add).then_inc(*lru_dve.inc("scan"))
                    D_("scan")
                    y = flat(ACC[:, bass.ds(c, 1), :])
                    v.tensor_tensor(y, s1, GG[:, :], ALU.mult).then_inc(*lru_dve.inc("y"))
                    D_("y")
                    v.tensor_tensor(s0, y, y, ALU.mult).then_inc(*lru_dve.inc("sq"))
                    D_("sq")
                    v.tensor_tensor(S[2][:, 0:T], S[2][:, 0:T], s0, ALU.add).then_inc(*lru_dve.inc("ss"))
                dv.wait_ge(*ln_act.at("std", l))
                s3 = S[3][:, 0:T]
                v.reciprocal(s3, s3).then_inc(*ln_dve.inc("rstd"))
                dv.wait_ge(*ln_dve.at("rstd", l))
                for c in range(LRU_CH):
                    v.scalar_tensor_tensor(out=ACC[:, c, :], in0=ACC[:, c, :], scalar=col(OUT_NORM + c), in1=s3,
                                           op0=ALU.mult, op1=ALU.mult).then_inc(*ln_dve.inc(f"y{c}"))
                with dv.Fori(0, HEADS) as h:
                    k = l * HEADS + h
                    D_ = lambda nm: dv.wait_ge(*hd_dve.at(nm, k))
                    s0, s1, s2 = S[0][:, 0:T], S[1][:, 0:T], S[2][:, 0:T]

                    def rope(ps, e):
                        v.tensor_tensor(tt(s0), ps, tt(R), ALU.mult).then_inc(*hd_dve.inc(f"{e}ev"))
                        D_(f"{e}ev")
                        v.tensor_tensor(s1, s0, COS[:, 0:T], ALU.mult).then_inc(*hd_dve.inc(f"{e}c"))
                        for j in range(4):
                            a, b = 32 * j, 32 * (j ^ 1)
                            v.tensor_tensor(S[2][a:a + 32, 0:T], S[0][b:b + 32, 0:T], SIN[b:b + 32, 0:T],
                                            ALU.mult).then_inc(*hd_dve.inc(f"{e}s{j}"))
                        D_(f"{e}s3")
                        v.tensor_tensor(s0, s1, s2, ALU.add).then_inc(*hd_dve.inc(f"{e}f"))

                    def lo(nm, dst, r0, d0, m, hi):
                        v.tensor_tensor(dst[d0:d0 + 64, m, :], S[0][r0:r0 + 64, 0:T], hi[r0:r0 + 64, m, :].bitcast(F32),
                                        ALU.subtract).then_inc(*hd_dve.inc(nm))

                    dv.wait_ge(*hd_pe.at("q", k))
                    rope(AT, "q")
                    dv.wait_ge(*hd_act.at("qh1", k))
                    lo("ql0", QS, 0, 64, 0, QS)
                    lo("ql1", QS, 64, 0, 1, QS)
                    dv.wait_ge(*hd_pe.at("k", k))
                    D_("ql1")
                    rope(BT, "k")
                    dv.wait_ge(*hd_act.at("kh3", k))
                    lo("kl0", KL, 0, 0, 0, KH)
                    lo("kl1", KL, 0, 64, 0, KH)
                    lo("kl2", KL, 64, 64, 1, KH)
                    lo("kl3", KL, 64, 0, 1, KH)
                    dv.wait_ge(*hd_pe.at("v", k))
                    D_("kl3")
                    v.tensor_tensor(tt(s0), AT, tt(R), ALU.mult).then_inc(*hd_dve.inc("vev"))
                    v.memset(VH[:, 0, :].bitcast(F32), 0.0).then_inc(*hd_dve.inc("vz"))
                    v.memset(VL[:, 0, :].bitcast(F32), 0.0).then_inc(*hd_dve.inc("vzl"))
                    for r, (ps, b0, nb) in enumerate(((M6, 1, 4), (M7, 5, 4), (M6, 0, 1))):
                        rows = META if r == 2 else P
                        dv.wait_ge(*hd_act.at(f"vh{r}", k))
                        if r == 2:
                            D_("vzl")
                        v.tensor_tensor(VL[0:rows, b0:b0 + nb, :], ps[0:rows, 0:nb * P].rearrange("p (a b) -> p a b", b=P),
                                        VH[0:rows, b0:b0 + nb, :].bitcast(F32), ALU.subtract).then_inc(*hd_dve.inc(f"vl{r}"))

                    def maxima(i):
                        keys = META + P * i
                        for mp, ps in ((0, AF), (1, BFL)):
                            mx, nb = (("mx", "nb"), ("my", "nc"))[mp]
                            dv.wait_ge(*hd_pe.at(f"s{i}{'ab'[mp]}", k))
                            v.tensor_reduce(SM[:, 32 + mp:33 + mp], ps[:, 0:keys], AX_X, ALU.max).then_inc(*hd_dve.inc(f"{mx}{i}"))
                            D_(f"{mx}{i}")
                            v.tensor_scalar(SM[:, 34 + mp:35 + mp], SM[:, 32 + mp:33 + mp], -(DH ** -0.5), None,
                                            ALU.mult).then_inc(*hd_dve.inc(f"{nb}{i}"))

                    maxima(0)
                    for i in range(NQ):
                        keys = META + P * i
                        p1, p2 = S[2 * (i % 2)][:, 0:keys], S[2 * (i % 2) + 1][:, 0:keys]
                        dv.wait_ge(*hd_act.at(f"q{i}", k))
                        v.reciprocal(SM[:, 40:42], SM[:, 36 + 2 * (i % 2):38 + 2 * (i % 2)]).then_inc(*hd_dve.inc(f"r{i}"))
                        D_(f"r{i}")
                        v.tensor_tensor(SM[:, 42:43], SM[:, 41:42], col(NEG_LAM), ALU.mult).then_inc(*hd_dve.inc(f"u{i}"))
                        v.tensor_scalar(p1, p1, SM[:, 40:41], None, ALU.mult).then_inc(*hd_dve.inc(f"w{i}"))
                        D_(f"w{i}")
                        v.scalar_tensor_tensor(out=p1, in0=p2, scalar=SM[:, 42:43], in1=p1, op0=ALU.mult,
                                               op1=ALU.add).then_inc(*hd_dve.inc(f"x{i}"))
                        if i == 0:
                            v.memset(S[0][:, META:P], 0.0).then_inc(*hd_dve.inc("z0"))
                        if i + 1 < NQ:
                            maxima(i + 1)
                        for r, blocks in enumerate(rounds(i)):
                            dv.wait_ge(*hd_act.at(f"th{i}_{r}", k))
                            b0, nb = blocks[0], len(blocks)
                            v.tensor_tensor(PTL[:, b0:b0 + nb, :], M6[:, 0:nb * P].rearrange("p (a b) -> p a b", b=P),
                                            PTH[:, b0:b0 + nb, :].bitcast(F32), ALU.subtract).then_inc(*hd_dve.inc(f"tl{i}_{r}"))
                    dv.wait_ge(*hd_act.at("std", k))
                    v.reciprocal(s1, s1).then_inc(*hd_dve.inc("rstd"))
                    D_("rstd")
                    y = flat(ACC[:, bass.ds(h + 4, 1), :])
                    v.scalar_tensor_tensor(out=y, in0=y, scalar=col(HEAD_GAIN), in1=s1, op0=ALU.mult,
                                           op1=ALU.mult).then_inc(*hd_dve.inc("y"))
                dv.wait_ge(*hd_dve.at("y", l * 4 + 3))
                dv.wait_ge(*hd_pe.at("stat", l * 4 + 3))
                v.tensor_tensor(HRES[:, :, :], HH[:, :, :].bitcast(F32), HL[:, :, :].bitcast(F32),
                                ALU.add).then_inc(*ysp_dve.inc("res"))
                v.memset(S[2][:, 0:T], 0.0).then_inc(*ysp_dve.inc("zero"))
                for c in range(DC):
                    dv.wait_ge(*ysp_act.at(f"h{c}", l))
                    v.tensor_tensor(HL[:, c, :], ACC[:, c, :], HH[:, c, :].bitcast(F32),
                                    ALU.subtract).then_inc(*ysp_dve.inc(f"l{c}"))
                with dv.Fori(0, DC // 2) as m:
                    for j in range(2):
                        kk = l * 4 + m
                        dv.wait_ge(*wo_act.at(f"sq{j}", kk))
                        dv.wait_ge(*(wo_dve.at("ss1", kk - 1) if j == 0 else wo_dve.at("ss0", kk)))
                        v.tensor_tensor(S[2][:, 0:T], S[2][:, 0:T], S[j][:, 0:T], ALU.add).then_inc(*wo_dve.inc(f"ss{j}"))

                def mix(Bd, r2, ss, gain, ffn):
                    dv.wait_ge(*Bd[1].at("std", l))
                    v.reciprocal(r2, r2).then_inc(*Bd[2].inc("rstd"))
                    v.memset(ss, 0.0).then_inc(*Bd[2].inc("zero"))
                    dv.wait_ge(*Bd[2].at("zero", l))
                    dv.sem_inc(past_dve, 1)
                    with dv.Fori(0, 4) as c2:
                        kk = l * 4 + c2
                        M_ = lambda nm, q=kk: dv.wait_ge(*Bd[3].at(nm, q))
                        ch = [bass.ds(c2 * 2 + j, 1) for j in range(2)]
                        for j in range(2):
                            a = flat(ACC[:, ch[j], :])
                            if ffn:
                                res = S[2 + j][:, 0:T]
                                v.tensor_tensor(res, flat(HH[:, ch[j], :]).bitcast(F32), flat(HL[:, ch[j], :]).bitcast(F32),
                                                ALU.add).then_inc(*Bd[3].inc(f"res{j}"))
                            else:
                                res = flat(HRES[:, ch[j], :])
                            v.scalar_tensor_tensor(out=a, in0=a, scalar=col(c2 * 2 + (gain + j)), in1=r2, op0=ALU.mult,
                                                   op1=ALU.mult).then_inc(*Bd[3].inc(f"t{j}"))
                            M_(f"t{j}")
                            v.tensor_tensor(a, a, res, ALU.add).then_inc(*Bd[3].inc(f"hn{j}"))
                        for j in range(2):
                            dv.wait_ge(*Bd[4].at(f"hh{j}", kk))
                            v.tensor_tensor(flat(HL[:, ch[j], :]), flat(ACC[:, ch[j], :]), flat(HH[:, ch[j], :]).bitcast(F32),
                                            ALU.subtract).then_inc(*Bd[3].inc(f"hl{j}"))
                            dv.wait_ge(*Bd[4].at(f"sq{j}", kk))
                            M_(*(("ss1", kk - 1) if j == 0 else ("ss0",)))
                            v.tensor_tensor(ss, ss, S[j][:, 0:T], ALU.add).then_inc(*Bd[3].inc(f"ss{j}"))
                    dv.wait_ge(*Bd[6].at("std", l))
                    v.reciprocal(R, R).then_inc(*Bd[7].inc("rstd"))

                mix(Wb, S[3][:, 0:T], S[2][:, 0:T], MIX_POST, False)
                dv.wait_ge(*Wb[7].at("rstd", l))

                def up(g, fs):
                    kk = l * NG + g
                    D_ = lambda nm: dv.wait_ge(*up_dve.at(nm, kk))
                    s1, s2, s3 = S[1][:, 0:T], S[2][:, 0:T], S[3][:, 0:T]
                    for j in range(G):
                        v.memset(S[0][:, 0:2], 0.0).then_inc(*up_dve.inc(f"pad{j}"))
                        dv.wait_ge(*up_pe.at(f"g{j}", kk))
                        v.tensor_tensor(tt(S[0][:, 2:2 + T]), AT, tt(R), ALU.mult).then_inc(*up_dve.inc(f"ev{j}"))
                        dv.wait_ge(*up_act.at(f"c2{j}", kk))
                        D_(f"ev{j}")
                        for q, nm, prev in ((1, "c1", "ev"), (0, "c0", "c1")):
                            D_(f"{prev}{j}")
                            v.scalar_tensor_tensor(out=s1, in0=S[0][:, q:q + T], scalar=col(g * 2 + (FCONV_W + 24 * q + j)),
                                                   in1=s1, op0=ALU.mult, op1=ALU.add).then_inc(*up_dve.inc(f"{nm}{j}"))
                        dv.wait_ge(*up_act.at(f"ge{j}", kk))
                        v.tensor_tensor(s2, s2, R, ALU.mult).then_inc(*up_dve.inc(f"gr{j}"))
                        D_(f"gr{j}")
                        dv.wait_ge(*up_pe.at(f"v{j}", kk))
                        v.tensor_tensor(tt(s3), tt(s2), BT, ALU.mult).then_inc(*up_dve.inc(f"f{j}"))
                        dv.wait_ge(*up_act.at(f"fh{j}", kk))
                        v.tensor_tensor(FL[:, fs + j, :], s3, FH[:, fs + j, :].bitcast(F32),
                                        ALU.subtract).then_inc(*up_dve.inc(f"fl{j}"))

                def down(g, first=False):
                    kk = l * NG + g
                    for m in range(DC):
                        ps, a = (AT, BT)[m % 2], ACC[:, m, :].rearrange("p (a b) -> p a b", a=NT)
                        dv.wait_ge(*dn_pe.at(f"m{m}", kk))
                        if first:
                            v.tensor_copy(a, ps).then_inc(*dn_dve.inc(f"a{m}"))
                        else:
                            dv.wait_ge(*dn_dve.at(f"a{m}", kk - 1))
                            v.tensor_tensor(a, a, ps, ALU.add).then_inc(*dn_dve.inc(f"a{m}"))

                up(0, 0)
                up(1, 2)
                down(0, first=True)
                with dv.Fori(1, NG // 2) as g2:
                    up(g2 * 2, 0)
                    down(g2 * 2 - 1)
                    up(g2 * 2 + 1, 2)
                    down(g2 * 2)
                ssl = Lb[4][:, :]
                v.memset(ssl, 0.0).then_inc(*ps_dve.inc("zero"))
                kk = l * NG + NG - 1
                for m in range(DC + 1):
                    if m < DC:
                        dv.wait_ge(*dn_pe.at(f"m{m}", kk))
                        a = ACC[:, m, :].rearrange("p (a b) -> p a b", a=NT)
                        dv.wait_ge(*dn_dve.at(f"a{m}", kk - 1))
                        v.tensor_tensor(a, a, (AT, BT)[m % 2], ALU.add).then_inc(*dn_dve.inc(f"a{m}"))
                    if m >= 1:
                        dv.wait_ge(*ps_act.at(f"sq{m - 1}", l))
                        dv.wait_ge(*ps_dve.at("zero" if m == 1 else f"ss{m - 2}", l))
                        v.tensor_tensor(ssl, ssl, Lb[(m - 1) % 2][:, :], ALU.add).then_inc(*ps_dve.inc(f"ss{m - 1}"))
                mix(Fb, Lb[5][:, :], ssl, FFN_POST, True)


LAMBDA_INIT = [0.8 - 0.6 * 2.718281828459045 ** (-0.3 * l) for l in range(L)]

NAMES = ["x", "meta_tokens", "ln_mix_pre", "ln_mix_post", "ln_ffn_pre", "ln_ffn_post", "w_in", "lru_conv_w",
         "lru_conv_b", "lru_wa", "lru_ba", "lru_wx", "lru_bx", "lru_a_param", "lru_out_norm", "lam_q1", "lam_k1",
         "lam_q2", "lam_k2", "diff_subln", "w_out", "w_up", "ffn_conv_w", "ffn_conv_b", "w_down"]


def rope_tables():
    import numpy as np
    inv = 1.0 / (np.float32(10000.0) ** (np.arange(0, DH, 2, dtype=np.float32) / np.float32(DH)))
    ang = inv.astype(np.float32)[:, None] * np.arange(T, dtype=np.float32)[None, :]
    cos, sin = np.cos(ang).astype(np.float32), np.sin(ang).astype(np.float32)
    return np.tile(cos, (4, 1)), np.concatenate([sin, -sin, sin, -sin], 0)


def kernel(**inputs):
    import numpy as np
    import concourse.bacc as bacc
    from concourse.bass_utils import run_bass_kernel_spmd

    nc = bacc.Bacc("TRN2", target_bir_lowering=False, num_devices=1)
    cos, sin = rope_tables()
    arrays = {n: np.ascontiguousarray(inputs[n]) for n in NAMES}
    arrays |= {"cos": cos, "sin": sin}
    t = {n: nc.dram_tensor(f"in_{n}", a.shape, F32, kind="ExternalInput").ap() for n, a in arrays.items()}
    out = nc.dram_tensor("out", (1, SEQ, D), F32, kind="ExternalOutput").ap()
    trunk(nc, t, out)
    r = run_bass_kernel_spmd(nc, [{f"in_{n}": a for n, a in arrays.items()}], core_ids=[0])
    return r.results[0]["out"]
```

```python
import concourse.bass as bass
from concourse import mybir
from contextlib import ExitStack

F32 = mybir.dt.float32
F32R = mybir.dt.float32r
ACT = mybir.ActivationFunctionType
ALU = mybir.AluOpType
AX_X = mybir.AxisListType.X

P = 128
L, D, SEQ, META = 2, 1024, 1024, 16
DC = D // P
TOK = META + SEQ
NT, TW = 3, 348
T = NT * TW
LRU_CH, HEADS, DH = 4, 4, 64
FF, FC = 3072, 24
G = 2
NG = FC // G
NQ = 9
TILES = 3 * LRU_CH + 3 * HEADS + DC + FC * 3
BF = DC * T * 4

MIX_PRE, MIX_POST, FFN_PRE, FFN_POST = 0, 8, 16, 24
CONV_W, CONV_B, GATE_BA, GATE_BX, A_PAR, OUT_NORM, SUBLN, LAM = 32, 48, 52, 56, 60, 64, 68, 69
FCONV_W, FCONV_B = 128, 128 + 72
NEG_C, NPAR = 224, 256
POS_C, NEG_LAM, HEAD_GAIN = 228, 232, 233


class Steps:

    def __init__(self, sem, names):
        self.sem, self.names, self.n = sem, names, 0

    def inc(self, name):
        assert self.names[self.n % len(self.names)] == name, (name, self.names[self.n % len(self.names)])
        self.n += 1
        return self.sem, 1

    def at(self, name, k):
        return self.sem, k * len(self.names) + (2 * len(self.names) + self.names.index(name) + 1)


class Parts:

    def __init__(self, *parts):
        self.parts = {n: p for p in parts for n in p.names}

    def inc(self, name):
        return self.parts[name].inc(name)

    def at(self, name, k):
        return self.parts[name].at(name, k)


def trunk(nc, t, out):
    ctx = ExitStack()
    with ctx:
        base = (nc.sbuf_base + 63) // 64 * 64

        def at(name, off, shape, dt=F32):
            return nc.alloc_sbuf_tensor_at(name, [P, *shape], dt, offset=base + off)

        HH = at("h_hi", 0, [DC, T], F32R)
        HL = at("h_lo", BF, [DC, T], F32R)
        OUTB = at("out_tok", 0, [SEQ // P, D])
        HSUM = at("h_sum", BF, [DC, T])
        ACC = at("acc", 2 * BF, [DC, T])
        o = 3 * BF
        RAW = [at(f"raw{i}", o + 4096 * i, [DC, P]) for i in range(2)]
        o += 8192
        SLOT = o
        WH = [at(f"w_hi{i}", SLOT + 8192 * i, [DC, P], F32R) for i in range(4)]
        WL = [at(f"w_lo{i}", SLOT + 8192 * i + 4096, [DC, P], F32R) for i in range(4)]
        BDH = at("bd_hi", SLOT + 16384, [2, P], F32R)
        BDL = at("bd_lo", SLOT + 16384 + 1024, [2, P], F32R)
        VV = at("v_parts", SLOT + 16384, [NQ, 2, P], F32R)
        PTH = at("pt_hi", SLOT + 16384 + 9216, [NQ, P], F32R)
        PTLA = at("pt_lo_a", SLOT + 16384 + 13824, [3, P], F32R)
        OT = [at(f"o_tok{i}", SLOT + 16384 + 15360 + 512 * i, [P]) for i in range(2)]
        o += 32768
        REG = o
        FH = at("f_hi", REG, [4, T], F32R)
        FL = at("f_lo", REG + 4 * T * 4, [4, T], F32R)
        HRES = at("h_res", REG, [DC, T])
        CH = [HRES[:, i, :] for i in range(DC)]
        XPAD = at("x_pad", REG, [T + 3])
        XC = at("x_conv", REG + 4192, [T])
        XH = at("x_hi", REG + 8384, [T], F32R)
        XL = at("x_lo", REG + 12576, [T], F32R)
        GG = at("gate", REG + 16768, [T])
        RA = at("r_a", REG + 20960, [T])
        IB = at("i_b", REG + 25152, [T])
        QKH = at("qk_hi", REG, [2, T], F32R)
        QKL = at("qk_lo", REG + 8352, [2, T], F32R)
        QKN = at("qk_next", REG + 16704, [2, T])
        VN = at("v_next", REG + 25056, [T])
        PTLB = at("pt_lo_b", REG + 29248, [6, P], F32R)
        OSQ = at("o_square", REG + 32320, [P])
        o += BF
        S = [at(f"s{i}", o + 4192 * i, [T + 4]) for i in range(4)]
        XIN = [at(f"x_in{i}", o + 4192 * i, [D]) for i in range(4)]
        XYZ = at("rope", o + 3 * 4192, [3, TW])
        XYZ0 = at("rope0", o, [3, TW])
        ROWS = at("rows", REG, [L, 2, P])
        o += 4 * 4192
        RSTD = at("rstd", o, [T]); o += 4192
        COS = at("cos", o, [T]); o += 4192
        SIN = at("sin", o, [T]); o += 4192
        IDENT = at("ident", o, [P + 64]); o += 768
        ONES = at("ones", o, [P]); o += 512
        MASK = at("mask", o, [64]); o += 256
        BD = at("bd_raw", o, [2, P]); o += 1024
        PAR = at("par", o, [L + 1, NPAR]); o += (L + 1) * NPAR * 4
        GP = at("ffn_post", o, [DC]); o += 64
        CUR = at("cur", o, [NPAR]); o += NPAR * 4
        SM = at("small", o, [64]); o += 256
        CST = at("cst", o, [8]); o += 64
        assert base + o <= nc.sbuf_usable_end, (base + o, nc.sbuf_usable_end)

        A = ctx.enter_context(nc.psum_tensor("psum_a", [P, NT, 512], F32))
        B = ctx.enter_context(nc.psum_tensor("psum_b", [P, NT, 512], F32))
        M6 = ctx.enter_context(nc.psum_tensor("psum_m6", [P, 512], F32))
        M7 = ctx.enter_context(nc.psum_tensor("psum_m7", [P, 512], F32))
        AT, BT = A[:, :, 0:TW], B[:, :, 0:TW]
        AF = A[:, :, :].rearrange("p a b -> p (a b)")
        BFL = B[:, :, :].rearrange("p a b -> p (a b)")

        BANKS = [M6, M7] + [A[:, i, :] for i in range(NT)] + [B[:, i, :] for i in range(NT)] + [M6]

        EIGHT = [A[:, i, :] for i in range(NT)] + [B[:, i, :] for i in range(NT)] + [M6, M7]

        def tt(ap):
            return ap.rearrange("p (a b) -> p a b", a=NT)

        def col(i):
            return CUR[:, i:i + 1] if isinstance(i, int) else CUR[:, bass.ds(i, 1)]

        EPS_D, ONE = CST[:, 0:1], CST[:, 2:3]
        MINUS_HALF, HEAD_EPS = CST[:, 6:7], CST[:, 7:8]

        every = []

        def steps(name, names):
            s = Steps(ctx.enter_context(nc.semaphore(name)), names)
            every.append((name.rsplit("_", 1)[1], s))
            return s

        def ahead(eng, which):
            for owner, s in every:
                if owner == which:
                    eng.sem_inc(s.sem, 2 * len(s.names))

        def sem(name):
            return ctx.enter_context(nc.semaphore(name))

        rows_zero, rows_in, const_in = sem("rows_zero"), sem("rows_in"), sem("const_in")
        out_done = sem("out_done")
        start_dve, start_act, start_pe = sem("start_dve"), sem("start_act"), sem("start_pe")
        x_in = [sem(f"x_in{i}") for i in range(4)]
        x_pe, x_act = sem("x_pe"), sem("x_act")
        raw_in = [sem("raw0_in"), sem("raw1_in"), sem("bd_in")]
        w_ready, w_chain = sem("w_ready"), sem("w_chain")
        q_half, q_chain = sem("q_half"), sem("q_chain")
        cur_ready = sem("cur_ready")
        past_pe, past_dve, past_po = sem("past_pe"), sem("past_dve"), sem("past_po")
        lru_pe = steps("lru_pe", ["x", "g", "r", "i"])
        lru_dve = steps("lru_dve", ["pad", "xev", "c2", "c1", "c0", "xcl", "gev", "ix", "a2", "m2",
                                    "b", "scan", "y", "sq", "ss"])
        lru_act = steps("lru_act", ["c3", "xch", "gg", "r", "i", "t", "a", "m"])
        STAT, STD, INV = ([f"{x}{i}" for i in range(NT)] for x in ("stat", "std", "rstd"))
        ln_pe, ln_act = steps("lrunorm_pe", STAT), steps("lrunorm_act", STD)
        ln_dve = steps("lrunorm_dve", ["zero"] + INV + ["y0", "y1", "y2", "y3"])

        def rounds(i):
            a0 = 5 if i == NQ - 2 else 7
            r = [range(0, min(3, i + 1)), range(3, min(a0, i + 1)), range(a0, i + 1)]
            return [list(b) for b in r if len(b)]

        def columns(i):
            keys = META + P * i
            if i == 0:
                return 512 - META, [(0, META)]
            if keys <= 512:
                return 512, [(0, keys)]
            if keys <= 1024:
                return 1024 - keys // 2, [(0, keys // 2), (keys // 2, keys)]
            return 272, [(0, 240), (240, 752), (752, keys)]

        pj_pe = steps("proj_pe", [f"u{u}" for u in range(9)])
        pj_dve = steps("proj_dve", [f"{x}{u}" for u in range(9) for x in (("ev", "sn") if u < 6 else ("ev",))])
        pj_act = steps("proj_act", [f"z{u}_{j}" for u in range(6) for j in range(4)])
        pj_po = steps("proj_pool", [f"{x}{u}" for u in range(6) for x in ("cs", "ad")])

        qk_act, qk_dve = steps("qk_act", ["qh", "kh"]), steps("qk_dve", ["ql", "kl"])
        open_pe, open_act = steps("open_pe", ["s0a", "s0b", "vt"]), steps("open_act", ["p0", "q0", "vh", "vm"])
        open_dve = steps("open_dve", ["mx0", "nb0", "my0", "nc0", "vz", "r0", "u0", "x0", "z0", "vl", "vm"])
        h_pe, h_act, h_dve = [], [], []
        for i in range(NQ):
            n, nr, more = i + 1, len(rounds(i)), i + 1 < NQ
            h_pe += [f"t{i}_0"] + ([f"t{i}_1"] if nr > 1 else [])
            h_act += [f"th{i}_0"] + ([f"th{i}_1"] if nr > 1 else [])
            h_dve += [f"tl{i}_0"] + ([f"tl{i}_1"] if nr > 1 else [])
            h_act += [f"oa{i - 1}"] if i else []
            if more:
                h_pe += [f"s{n}a"]
                h_act += [f"p{n}"]
                h_dve += [f"mx{n}", f"nb{n}"]
            h_dve += [f"ob{i - 1}"] if i else []
            if nr > 2:
                h_pe += [f"t{i}_2"]
                h_act += [f"th{i}_2"]
                h_dve += [f"tl{i}_2"]
            h_act += [f"sq{i - 1}"] if i else []
            if more:
                h_pe += [f"s{n}b"]
                h_act += [f"q{n}"]
                h_dve += [f"my{n}", f"nc{n}"]
            if i >= 2:
                h_pe += [f"ot{i - 2}"]
                h_act += [f"oc{i - 2}"]
                h_dve += [f"sc{i - 2}"]
            h_pe += [f"pv{i}"]
            h_dve += [f"r{n}", f"u{n}", f"x{n}"] if more else []
        h_pe += ["ot7", "ot8"]
        h_act += ["oa8", "sq8", "oc7", "oc8"]
        h_dve += ["ob8", "sc7", "sc8"]
        hd_po = steps("head_pool", [f"{x}{i}" for i in range(NQ) for x in ("e", "rn")])
        hd_pe, hd_dve, hd_act = (Parts(open_pe, steps("head_pe", h_pe)), Parts(open_dve, steps("head_dve", h_dve)),
                                 Parts(open_act, steps("head_act", h_act)))
        LAST_TL = [f"tl{i}_{len(rounds(i)) - 1}" for i in range(NQ)]

        tail_act = steps("tail_act", [f"h{c}" for c in range(DC)])
        tail_po, tail_dve = steps("tail_pool", [f"l{c}" for c in range(DC - 1)]), steps("tail_dve", ["zero", "l7"])
        res_out, res_in = sem("stream_stored"), sem("stream_loaded")

        wo_pe = steps("wout_pe", ["m0", "m1"])
        wo_act = steps("wout_act", ["y0", "sq0", "y1", "sq1"])
        wo_dve = steps("wout_dve", ["ss0", "ss1"])

        def boundary(name):
            return (steps(name + "post_pe", STAT), steps(name + "post_act", STD), steps(name + "post_dve", INV),
                    steps(name + "mix_dve", [f"{x}{c}" for c in range(DC) for x in ("t", "hn")]))

        def entry(name):
            return (steps(name + "in_pe", [f"st{c}" for c in range(DC - 1)] + STAT),
                    steps(name + "in_act", [f"{x}{c}" for c in range(DC) for x in ("hh", "sq")] + STD),
                    steps(name + "in_pool", [f"hl{c}" for c in range(DC)]), steps(name + "in_dve", INV))

        Wb, Fb = boundary("w"), boundary("f")
        Me, Fe = entry("m"), entry("f")
        fr_po = steps("ffnres_pool", [f"r{c}" for c in range(DC)])
        gp_dve = steps("gain_dve", ["copy"])
        up_pe = steps("up_pe", ["g0", "v0", "g1", "v1"])
        up_dve = steps("up_dve", [f"{x}{j}" for j in range(2) for x in ("pad", "ev", "c1", "c0", "gr", "f", "fl")])
        up_act = steps("up_act", [f"{x}{j}" for j in range(2) for x in ("c2", "ge", "fh")])
        dn_pe = steps("down_pe", [f"m{m}" for m in range(DC)])
        dn_dve = steps("down_dve", [f"a{m}" for m in range(DC)])
        ps_act = steps("postsq_act", [f"sq{m}" for m in range(DC)])
        ps_dve = steps("postsq_dve", ["zero"] + [f"ss{m}" for m in range(DC)])
        ep_pe, ep_act = sem("ep_pe"), sem("ep_act")

        block = ctx.enter_context(nc.Block())

        N_HEAD, N_WOUT, N_UP = 3 * LRU_CH, 3 * (LRU_CH + HEADS), 3 * (LRU_CH + HEADS) + DC
        W_CREDIT = 4

        def ready(n, l):
            return w_ready, l * TILES + n + (W_CREDIT + 1)

        @block.sync
        def _(sp):
            xt = t["x"][0].rearrange("(b p) d -> b p d", p=P)

            def tokens(b):
                if b >= 4:
                    sp.wait_ge(x_pe, b - 3)
                if b == 0:
                    sp.dma_start(XIN[0][0:META, :], t["meta_tokens"]).then_inc(x_in[0], 16)
                else:
                    sp.dma_start(XIN[b % 4][:, :], xt[b - 1]).then_inc(x_in[b % 4], 16)

            for b in range(4):
                tokens(b)
            sp.wait_ge(rows_zero, 1)

            def rows(r0, src, count, tl=0):
                sp.dma_start(ROWS[r0:r0 + count, :, tl, :], src.rearrange("l (r p) -> r l p", p=P)).then_inc(rows_in, 16)

            rows(MIX_PRE, t["ln_mix_pre"], 8)
            rows(MIX_POST, t["ln_mix_post"], 8)
            rows(FFN_PRE, t["ln_ffn_pre"], 8)
            rows(FFN_POST, t["ln_ffn_post"], 8)
            rows(CONV_W, t["lru_conv_w"].rearrange("l k c -> l (k c)"), 16)
            rows(CONV_B, t["lru_conv_b"], 4)
            rows(GATE_BA, t["lru_ba"].rearrange("l n c -> l (n c)"), 4)
            rows(GATE_BX, t["lru_bx"].rearrange("l n c -> l (n c)"), 4)
            rows(A_PAR, t["lru_a_param"], 4)
            rows(OUT_NORM, t["lru_out_norm"], 4)
            rows(SUBLN, t["diff_subln"], 1)
            rows(0, t["ffn_conv_w"].rearrange("l k c -> l (k c)"), 72, 1)
            rows(72, t["ffn_conv_b"], 24, 1)
            for i, nm in enumerate(("lam_q1", "lam_q2", "lam_k1", "lam_k2")):
                sp.dma_start(ROWS[LAM + i:LAM + i + 1, :, 0, 0:DH],
                             t[nm].rearrange("l (r p) -> r l p", r=1)).then_inc(rows_in, 16)
            for b in range(4, 9):
                tokens(b)
            sp.dma_start(COS[:, :], t["cos"]).then_inc(const_in, 16)
            sp.dma_start(SIN[:, :], t["sin"]).then_inc(const_in, 16)

            def load(dst, src, r, l, n, back):
                sp.wait_ge(*ready(n - back, l))
                sp.dma_start(dst, src).then_inc(raw_in[r], 16)

            w_in = t["w_in"].rearrange("l (k p) n -> l p k n", p=P)
            w_out = t["w_out"].rearrange("l (k p) n -> l p k n", p=P)
            w_up = t["w_up"].rearrange("l (k p) n -> l p k n", p=P)
            w_dn = t["w_down"].rearrange("l (g p) (m n) -> l g p m n", p=P, n=P)

            def sl(w, l, c0):
                return w[bass.ds(l, 1), :, :, bass.ds(c0, P)].rearrange("a p k n -> p (a k) n")

            def dn(l, g):
                return w_dn[bass.ds(l, 1), bass.ds(g, 1)].rearrange("a b p m n -> p (a b m) n")

            sp.wait_ge(rows_zero, 2)
            with sp.Fori(0, L) as l:
                def lru(c):
                    load(RAW[0][:], sl(w_in, l, c * P), 0, l, c * 3, 2)
                    load(RAW[1][:], sl(w_in, l, c * P + 512), 1, l, c * 3 + 1, 2)
                    sp.wait_ge(*ready(c * 3 + 2 - 3, l))
                    for j, nm in enumerate(("lru_wa", "lru_wx")):
                        for e in range(2):
                            src = t[nm].rearrange("l (c e) a b -> l c e a b", e=2)
                            src = src[bass.ds(l, 1), bass.ds(c, 1), e].rearrange("x y a b -> a (x y) b")
                            sp.dma_start(BD[64 * e:64 * e + 64, j:j + 1, 64 * e:64 * e + 64], src).then_inc(raw_in[2], 16)

                lru(0)
                sp.wait_ge(x_act, 9)
                sp.wait_ge(*Fb[3].at("hn7", l - 1))
                sp.dma_start(t["stream"].rearrange("p (c t) -> p c t", t=T), ACC[:, :, :]).then_inc(res_out, 16)
                with sp.Fori(1, LRU_CH) as c:
                    lru(c)
                with sp.Fori(0, HEADS) as h:
                    load(RAW[0][:], sl(w_in, l, h * P + 1024), 0, l, h * 3 + N_HEAD, 1)
                    load(RAW[1][:], sl(w_in, l, h * P + 1536), 1, l, h * 3 + (N_HEAD + 1), 3)
                    load(RAW[0][:], sl(w_in, l, h * P + 2048), 0, l, h * 3 + (N_HEAD + 2), 2)
                load(RAW[0][:], sl(w_out, l, 0), 0, l, N_WOUT, 1)
                load(RAW[1][:], sl(w_out, l, P), 1, l, N_WOUT + 1, 2)
                load(RAW[0][:], sl(w_out, l, 2 * P), 0, l, N_WOUT + 2, 2)
                load(RAW[1][:], sl(w_out, l, 3 * P), 1, l, N_WOUT + 3, 2)
                sp.wait_ge(*tail_dve.at("l7", l))
                sp.dma_start(HRES[:, :, :], t["stream"].rearrange("p (c t) -> p c t", t=T)).then_inc(res_in, 16)
                with sp.Fori(2, DC // 2) as m:
                    for j in range(2):
                        load(RAW[j][:], sl(w_out, l, m * 256 + P * j), j, l, m * 2 + (N_WOUT + j), 2)

                def up(g, n):
                    for j in range(G):
                        load(RAW[0][:], sl(w_up, l, g * 256 + P * j), 0, l, n + 2 * j, 2)
                        load(RAW[1][:], sl(w_up, l, g * 256 + (FF + P * j)), 1, l, n + (2 * j + 1), 2)

                def down(g, n):
                    for j in range(G):
                        load(RAW[j][:], dn(l, g * G + j), j, l, n + j, 2)

                up(0, N_UP)
                with sp.Fori(1, NG) as g:
                    up(g, g * 6 + (N_UP - 2))
                    down(g - 1, g * 6 + (N_UP + 2))
                down(NG - 1, N_UP + 6 * NG - 2)
            ot = out[0].rearrange("(b p) d -> b p d", p=P)
            for e in range(2):
                for b in range(8):
                    sp.wait_ge(ep_act, 8 * e + b + 1)
                    sp.dma_start(ot[b][:, 512 * e:512 * e + 512], OUTB[:, b, 512 * e:512 * e + 512]).then_inc(out_done, 16)
            sp.wait_ge(out_done, 16 * 16)

        @block.gpsimd
        def _(po):
            nc.gpsimd.memset(ROWS[:], 0.0).then_inc(rows_zero, 1)
            nc.gpsimd.memset(BD[:], 0.0).then_inc(w_ready, W_CREDIT)
            nc.gpsimd.memset(MASK[:], -1e30).then_inc(w_chain, 1)
            nc.gpsimd.memset(ONES[:], 1.0).then_inc(rows_zero, 1)
            nc.gpsimd.memset(IDENT[:], 0.0).then_inc(w_chain, 1)
            po.wait_ge(w_chain, 2)
            nc.gpsimd.affine_select(out=IDENT[:], in_=IDENT[:], compare_op=ALU.not_equal, fill=1.0, base=0,
                                    pattern=[[-1, P + 64]], channel_multiplier=1).then_inc(w_chain, 1)
            C0 = 3
            CH = 2 * TILES

            def split(n, l, raw, hi, lo, gain):
                shape = [P, raw.shape[1], P]
                if gain is None:
                    g = ONE.rearrange("p (a b) -> p a b", a=1).to_broadcast(shape)
                else:
                    g = CUR[:, gain:gain + raw.shape[1]].rearrange("p (a b) -> p a b", b=1).to_broadcast(shape)
                nc.gpsimd.tensor_tensor(hi, raw, g, ALU.mult).then_inc(w_chain, 1)
                nc.gpsimd.tensor_tensor(raw, raw, g, ALU.mult).then_inc(w_chain, 1)
                po.wait_ge(w_chain, l * CH + n * 2 + (C0 + 2))
                nc.gpsimd.tensor_tensor(lo, raw, hi.bitcast(F32), ALU.subtract).then_inc(w_ready, 1)

            PER_LAYER = [LRU_CH + 2 * HEADS + DC // 2 + FC + FC // 2, LRU_CH + HEADS + DC // 2 + FC + FC // 2, LRU_CH]
            assert sum(PER_LAYER) == TILES

            def piece(n, l, r, count, slot, gain):
                per = PER_LAYER[r]
                step = 64 if r == 2 else 16
                po.wait_ge(raw_in[r], l * (per * step) + count * step + step)
                if r == 2:
                    split(n, l, BD[:], BDH[:], BDL[:], gain)
                else:
                    split(n, l, RAW[r][:], WH[slot][:], WL[slot][:], gain)

            ahead(po, "pool")
            po.wait_ge(start_dve, 1)
            with po.Fori(0, L) as l:
                po.wait_ge(cur_ready, l + 1)
                po.wait_ge(*dn_pe.at("m7", l * NG - 1))

                def split_stream(E):
                    for c in range(DC):
                        po.wait_ge(*E[1].at(f"hh{c}", l))
                        nc.gpsimd.tensor_tensor(HL[:, c, :], ACC[:, c, :], HH[:, c, :].bitcast(F32),
                                                ALU.subtract).then_inc(*E[2].inc(f"hl{c}"))

                def lru(c, first):
                    k = l * LRU_CH + c
                    if not first:
                        po.wait_ge(*lru_pe.at("x", k - 1))
                    piece(c * 3, l, 0, c, 0, MIX_PRE)
                    if first:
                        split_stream(Me)
                    po.wait_ge(*lru_pe.at("g", k - 1))
                    piece(c * 3 + 1, l, 1, c, 1, MIX_PRE)
                    po.wait_ge(*lru_pe.at("i", k - 1))
                    piece(c * 3 + 2, l, 2, c, 2, None)

                lru(0, True)
                po.sem_inc(past_po, 1)
                with po.Fori(1, LRU_CH) as c:
                    lru(c, False)
                po.wait_ge(*lru_pe.at("g", l * LRU_CH + 3))
                po.sem_inc(past_po, 1)

                def rope(u, k, xyz=XYZ):
                    e, t_ = divmod(u, 3)
                    tl = slice(TW * t_, TW * t_ + TW)
                    po.wait_ge(*pj_dve.at(f"sn{u}", k))
                    nc.gpsimd.tensor_tensor(xyz[:, 0, :], xyz[:, 0, :], COS[:, tl], ALU.mult).then_inc(*pj_po.inc(f"cs{u}"))
                    po.wait_ge(*pj_po.at(f"cs{u}", k))
                    po.wait_ge(*pj_act.at(f"z{u}_3", k))
                    po.wait_ge(*qk_dve.at("kl", k - 1))
                    nc.gpsimd.tensor_tensor(QKN[:, e, tl], xyz[:, 0, :], xyz[:, 2, :],
                                            ALU.add).then_inc(*pj_po.inc(f"ad{u}"))

                def piece_qk(h, k):
                    po.wait_ge(*pj_pe.at("u8", k - 1))
                    count, hf = h * 2 + 4, DC // 2
                    po.wait_ge(raw_in[0], l * (PER_LAYER[0] * 16) + count * 16 + 16)
                    raw, hi, lo = RAW[0][:, 0:hf, :], WH[0][:, 0:hf, :], WL[0][:, 0:hf, :]
                    g = CUR[:, MIX_PRE:MIX_PRE + hf].rearrange("p (a b) -> p a b", b=1).to_broadcast([P, hf, P])
                    nc.gpsimd.tensor_tensor(hi, raw, g, ALU.mult).then_inc(q_chain, 1)
                    nc.gpsimd.tensor_tensor(raw, raw, g, ALU.mult).then_inc(q_chain, 1)
                    po.wait_ge(q_chain, k * 2 + 2)
                    nc.gpsimd.tensor_tensor(lo, raw, hi.bitcast(F32), ALU.subtract).then_inc(q_half, 1)
                    split(h * 3 + N_HEAD, l, RAW[0][:, hf:DC, :], WH[0][:, hf:DC, :], WL[0][:, hf:DC, :], MIX_PRE + hf)
                    po.wait_ge(*pj_pe.at("u5", k - 1))
                    piece(h * 3 + (N_HEAD + 1), l, 1, h + 4, 1, MIX_PRE)

                def piece_v(h, k):
                    po.wait_ge(*pj_pe.at("u2", k))
                    piece(h * 3 + (N_HEAD + 2), l, 0, h * 2 + 5, 0, MIX_PRE)

                def norm(i, k):
                    po.wait_ge(*hd_act.at(f"sq{i}", k))
                    e = i % 2
                    po.wait_ge(*(hd_po.at(f"rn{i - 1}", k) if i else hd_po.at("rn8", k - 1)))
                    nc.gpsimd.tensor_tensor(SM[:, 50:51], SM[:, 46 + e:47 + e], HEAD_EPS,
                                            ALU.add).then_inc(*hd_po.inc(f"e{i}"))
                    po.wait_ge(*hd_po.at(f"e{i}", k))
                    nc.gpsimd.tensor_tensor(SM[:, 48 + e:49 + e], SM[:, 50:51], MINUS_HALF,
                                            ALU.pow).then_inc(*hd_po.inc(f"rn{i}"))

                def piece_out(m, j):
                    po.wait_ge(*wo_pe.at(f"m{j}", l * 4 + m - 1))
                    piece(m * 2 + (N_WOUT + j), l, j, m + (12 if j == 0 else 8), j, None)

                piece_qk(0, l * HEADS)
                piece_v(0, l * HEADS)
                for u in range(6):
                    rope(u, l * HEADS, (XYZ, XYZ0)[u % 2])
                with po.Fori(0, HEADS - 1) as h:
                    k = l * HEADS + h
                    piece_qk(h + 1, k + 1)
                    for i in range(NQ):
                        if i < 6:
                            rope(i, k + 1)
                        if i == 3:
                            piece_v(h + 1, k + 1)
                        norm(i, k)
                po.wait_ge(*pj_pe.at("u8", l * HEADS + 3))
                for i in range(NQ):
                    if 1 <= i <= 7:
                        c = i - 1
                        po.wait_ge(*tail_act.at(f"h{c}", l))
                        nc.gpsimd.tensor_tensor(HL[:, c, :], ACC[:, c, :], HH[:, c, :].bitcast(F32),
                                                ALU.subtract).then_inc(*tail_po.inc(f"l{c}"))
                    norm(i, l * HEADS + 3)
                    if i in (2, 4):
                        piece_out(0, i // 2 - 1)
                with po.Fori(1, DC // 2) as m:
                    for j in range(2):
                        piece_out(m, j)

                def up(g, n, c0, c1, prev):
                    for j in range(G):
                        for e, nm in enumerate(("g", "v")):
                            if prev is not None and j == 0:
                                po.wait_ge(*up_pe.at(f"{nm}1", prev))
                            if j == 1:
                                po.wait_ge(*up_pe.at(f"{nm}0", l * NG + g))
                            piece(n + (2 * j + e), l, e, (c0, c1)[e] + j, e, FFN_PRE)
                            if prev is None and j == 0 and e == 1:
                                split_stream(Fe)

                def down(g, n, c0, c1, final=False):
                    if not final:
                        po.wait_ge(*dn_pe.at("m7", l * NG + g - 1))
                    for j in range(G):
                        if final:
                            po.wait_ge(*up_pe.at(("g1", "v1")[j], l * NG + g))
                        piece(n + j, l, j, (c0, c1)[j], j if final else 2 + j, None)

                po.wait_ge(*wo_pe.at("m1", l * 4 + 3))
                up(0, N_UP, 16, 12, None)
                with po.Fori(1, NG) as g:
                    up(g, g * 6 + (N_UP - 2), g * 3 + 15, g * 3 + 11, l * NG + g - 1)
                    down(g - 1, g * 6 + (N_UP + 2), g * 3 + 17, g * 3 + 13)
                down(NG - 1, N_UP + 6 * NG - 2, 16 + 35, 12 + 35, True)
                po.wait_ge(*up_pe.at("v1", l * NG + NG - 1))
                for c in range(DC):
                    nc.gpsimd.tensor_tensor(HSUM[:, c, :], HH[:, c, :].bitcast(F32), HL[:, c, :].bitcast(F32),
                                            ALU.add).then_inc(*fr_po.inc(f"r{c}"))

        @block.tensor
        def _(pe):
            def product(ps, wh, wl, xh, xl, tiles=range(NT)):
                n = wh.shape[1]
                for t_ in tiles:
                    for c in range(n):
                        pe.matmul(ps[:, t_, 0:TW], wh[:, c, :], xh(c, t_), start=(c == 0), stop=False)
                        pe.matmul(ps[:, t_, 0:TW], wh[:, c, :], xl(c, t_), start=False, stop=False)
                        m = pe.matmul(ps[:, t_, 0:TW], wl[:, c, :], xh(c, t_), start=False, stop=(c == n - 1))
                return m

            def hs(w):
                return (lambda c, t_: HH[:, c, TW * t_:TW * t_ + TW]), (lambda c, t_: HL[:, c, TW * t_:TW * t_ + TW])

            def project(ps, slot):
                return product(ps, WH[slot], WL[slot], *hs(slot))

            def stat(ps, src, marks):
                for t_ in range(NT):
                    pe.matmul(ps[:, t_, 0:TW], ONES[:, :], src[:, TW * t_:TW * t_ + TW], start=True,
                              stop=True).then_inc(*marks.inc(STAT[t_]))

            ahead(pe, "pe")
            pe.wait_ge(w_chain, 3)

            def tokens(b):
                rows, buf = (META, 0) if b == 0 else (P, b % 4)
                ps = (A, B)[b % 2]
                pe.wait_ge(x_in[buf], 16 * (b // 4 + 1))
                if b >= 2:
                    pe.wait_ge(x_act, b - 1)
                for c in range(DC):
                    m = pe.transpose(ps[:, c // 4, (c % 4) * P:(c % 4) * P + rows],
                                     XIN[buf][0:rows, c * P:(c + 1) * P], IDENT[0:rows, 0:rows])
                m.then_inc(x_pe, 1)

            for b in range(4):
                tokens(b)
            pe.wait_ge(rows_in, 16 * 17)
            for l in range(L):
                for e in range(2):
                    m = pe.transpose(M6[:, (2 * l + e) * P:(2 * l + e + 1) * P], ROWS[:, l, e, :], IDENT[:, 0:P])
            m.then_inc(start_pe, 1)
            for b in range(4, 6):
                tokens(b)
            pe.wait_ge(rows_zero, 2)
            pe.wait_ge(start_dve, 3)
            pe.matmul(M7[:, 0:2 * L], ONES[:, :], SM[:, 0:2 * L], start=True, stop=True).then_inc(start_pe, 1)
            for b in range(6, 9):
                tokens(b)

            def enter(E, l, tile, mark):
                for c in range(DC):
                    pe.wait_ge(*E[1].at(f"sq{c}", l))
                    for t_ in range(NT):
                        m = pe.matmul(B[:, t_, 0:TW], ONES[:, :], S[c % 2][:, TW * t_:TW * t_ + TW], start=(c == 0),
                                      stop=(c == DC - 1))
                        if c == DC - 1:
                            m.then_inc(*E[0].inc(STAT[t_]))
                    if c < DC - 1:
                        m.then_inc(*E[0].inc(f"st{c}"))
                    if c == 0:
                        pe.wait_ge(*ready(tile, l))
                    pe.wait_ge(*E[2].at(f"hl{c}", l))
                    for t_ in range(NT):
                        xh, xl = HH[:, c, TW * t_:TW * t_ + TW], HL[:, c, TW * t_:TW * t_ + TW]
                        pe.matmul(A[:, t_, 0:TW], WH[0][:, c, :], xh, start=(c == 0), stop=False)
                        pe.matmul(A[:, t_, 0:TW], WH[0][:, c, :], xl, start=False, stop=False)
                        m = pe.matmul(A[:, t_, 0:TW], WL[0][:, c, :], xh, start=False, stop=(c == DC - 1))
                m.then_inc(*mark)

            with pe.Fori(0, L) as l:
                enter(Me, l, 0, lru_pe.inc("x"))
                pe.wait_ge(*Me[1].at("std2", l))

                def lru(c, first):
                    k = l * LRU_CH + c
                    if not first:
                        pe.wait_ge(*ready(c * 3, l))
                        pe.wait_ge(*lru_act.at("r", k - 1))
                        project(A, 0).then_inc(*lru_pe.inc("x"))
                    pe.wait_ge(*ready(c * 3 + 1, l))
                    pe.wait_ge(*lru_act.at("i", k - 1))
                    project(B, 1).then_inc(*lru_pe.inc("g"))
                    pe.wait_ge(*ready(c * 3 + 2, l))
                    pe.wait_ge(*lru_dve.at("xcl", k))
                    xs = (lambda c_, t_: XH[:, TW * t_:TW * t_ + TW]), (lambda c_, t_: XL[:, TW * t_:TW * t_ + TW])
                    product(A, BDH[:, 0:1, :], BDL[:, 0:1, :], *xs).then_inc(*lru_pe.inc("r"))
                    pe.wait_ge(*lru_dve.at("gev", k))
                    product(B, BDH[:, 1:2, :], BDL[:, 1:2, :], *xs).then_inc(*lru_pe.inc("i"))

                lru(0, True)
                pe.sem_inc(past_pe, 1)
                with pe.Fori(1, LRU_CH) as c:
                    lru(c, False)

                def unit(u, h, k, ps, chunks=range(DC)):
                    e, t_ = divmod(u, 3)
                    slot = e % 2
                    for c in chunks:
                        if u == 0 and c == 0:
                            pe.wait_ge(q_half, k + 1)
                        elif (u == 0 and c == DC // 2) or (t_ == 0 and e > 0 and c == 0):
                            pe.wait_ge(*ready(h * 3 + (N_HEAD + e), l))
                        xh, xl = HH[:, c, TW * t_:TW * t_ + TW], HL[:, c, TW * t_:TW * t_ + TW]
                        pe.matmul(ps[:, 0:TW], WH[slot][:, c, :], xh, start=(c == 0), stop=False)
                        pe.matmul(ps[:, 0:TW], WH[slot][:, c, :], xl, start=False, stop=False)
                        m = pe.matmul(ps[:, 0:TW], WL[slot][:, c, :], xh, start=False, stop=(c == DC - 1))
                    if c == DC - 1:
                        m.then_inc(*pj_pe.inc(f"u{u}"))

                def scores(i, mp, k):
                    q0, keys = (0, META) if i == 0 else (META + P * (i - 1), META + P * i)
                    ps = (AF, BFL)[mp]
                    if i == 0 and mp == 0:
                        pe.wait_ge(*qk_dve.at("kl", k))
                    if i == 1 and mp == 1:
                        pe.wait_ge(*hd_dve.at("vm", k))
                    pe.wait_ge(*hd_act.at(f"{'pq'[mp]}{i - 1}", k) if i else hd_act.at(f"{'pq'[mp]}8", k - 1))
                    if i == 1 and mp == 0:
                        pe.wait_ge(*hd_dve.at("vl", k))
                    if i == 0 and mp == 0:
                        pe.wait_ge(*hd_dve.at("tl8_1", k - 1))
                    elif i == 8 and mp == 0:
                        pe.wait_ge(*hd_dve.at("tl7_1", k))
                    elif i == 8:
                        pe.wait_ge(*hd_dve.at("ob6", k))
                    rows = slice(64 * mp, 64 * mp + 64)
                    c0, parts = columns(i)
                    m0 = keys - 64
                    for b0, b1 in parts:
                        masked = i >= 1 and b1 == keys
                        o_ = ps[:, c0 + b0:c0 + b1]
                        qh, ql = QKH[rows, 0, q0:q0 + P], QKL[rows, 0, q0:q0 + P]
                        pe.matmul(o_, qh, QKH[rows, 1, b0:b1], start=True, stop=False)
                        pe.matmul(o_, qh, QKL[rows, 1, b0:b1], start=False, stop=False)
                        m = pe.matmul(o_, ql, QKH[rows, 1, b0:b1], start=False, stop=not masked)
                        if masked:
                            m = pe.matmul(ps[:, c0 + m0:c0 + b1], IDENT[rows, 64 * mp:64 * mp + P], MASK[rows, :],
                                          start=False, stop=True)
                    m.then_inc(*hd_pe.inc(f"s{i}{'ab'[mp]}"))

                def opening(k):
                    scores(0, 0, k)
                    pe.wait_ge(*hd_dve.at("ob8", k - 1))
                    scores(0, 1, k)
                    pe.wait_ge(*pj_dve.at("ev8", k))
                    for b in range(NQ):
                        t0 = META + P * (b - 1) if b else 0
                        ps = AF[:, 512 + (b - 1) * P:512 + b * P] if b else B[:, 1, 0:P]
                        m = pe.transpose(ps, VN[:, t0:t0 + P], IDENT[:, 0:P])
                    m.then_inc(*hd_pe.inc("vt"))

                def head(k, early, late, following):
                    def turn(i, r):
                        if r == 0:
                            pe.wait_ge(*hd_dve.at("z0" if i == 0 else f"x{i}", k))
                        ps = (M7, A[:, 0, :], M7)[r]
                        if r == 2:
                            pe.wait_ge(*hd_dve.at(f"tl{i}_0", k))
                        elif r == 0 and i >= 3:
                            pe.wait_ge(*hd_act.at(f"oc{i - 3}", k))
                        elif r == 0:
                            pe.wait_ge(*(hd_dve.at(LAST_TL[i - 1], k) if i else hd_act.at("oc8", k - 1)))
                        for n, b in enumerate(rounds(i)[r]):
                            t0 = META + P * (b - 1) if b else 0
                            m = pe.transpose(ps[:, n * P:(n + 1) * P], S[i % 2][:, t0:t0 + P], IDENT[:, 0:P])
                        m.then_inc(*hd_pe.inc(f"t{i}_{r}"))

                    def turn_out(i):
                        pe.wait_ge(*hd_dve.at(f"sc{i}", k))
                        if i < 7:
                            pe.wait_ge(*hd_dve.at(f"tl{i + 2}_{2 if len(rounds(i + 2)) > 2 else 0}", k))
                        else:
                            pe.wait_ge(*hd_act.at(f"oc{i - 1}", k))
                        pe.transpose(M7[:, 3 * P:4 * P], OT[i % 2][:, :], IDENT[:, 0:P]).then_inc(*hd_pe.inc(f"ot{i}"))

                    for i in range(NQ):
                        turn(i, 0)
                        if len(rounds(i)) > 1:
                            turn(i, 1)
                        if i + 1 < NQ:
                            scores(i + 1, 0, k)
                        if len(rounds(i)) > 2:
                            turn(i, 2)
                        if i + 1 < NQ:
                            scores(i + 1, 1, k)
                        early(i)
                        if i >= 2:
                            turn_out(i - 2)
                        pe.wait_ge(*hd_dve.at(LAST_TL[i], k))
                        if i:
                            pe.wait_ge(*hd_dve.at(f"ob{i - 1}", k))
                        else:
                            pe.wait_ge(*hd_act.at("q0", k))
                        if i == 7:
                            pe.wait_ge(*hd_act.at("q8", k))
                        o_ = B[:, 0, 0:2 * P]
                        for b in range(i + 1):
                            ph, pl = PTH[:, b, :], PTLB[:, b - 3, :] if b >= 3 else PTLA[:, b, :]
                            vv = VV[:, b, :, :].rearrange("p a b -> p (a b)")
                            pe.matmul(o_, ph, vv, start=(b == 0), stop=False)
                            m = pe.matmul(o_, pl, vv, start=False, stop=(b == i))
                        m.then_inc(*hd_pe.inc(f"pv{i}"))
                        late(i)
                    following()
                    turn_out(7)
                    turn_out(8)

                for u in range(9):
                    if u == 2:
                        pe.wait_ge(*lru_act.at("r", l * 4 + 3))
                    elif u == 5:
                        pe.wait_ge(*lru_act.at("i", l * 4 + 3))
                    elif u == 8:
                        pe.wait_ge(*pj_dve.at("ev0", l * 4))
                    unit(u, 0, l * 4, BANKS[u])
                    if u == 6:
                        pe.wait_ge(*pj_dve.at("ev4", l * 4))
                        pe.wait_ge(*lru_dve.at("ss", l * 4 + 3))
                        stat(A, S[2], ln_pe)
                pe.wait_ge(*ln_act.at("std2", l))
                opening(l * HEADS)
                with pe.Fori(0, HEADS - 1) as h:
                    k = l * HEADS + h

                    def first_half(u):
                        pe.wait_ge(*(pj_dve.at(f"ev{u - 1}", k + 1) if u else pj_dve.at("ev8", k)))
                        unit(u, h + 1, k + 1, M6, range(0, DC // 2))

                    def second_half(u):
                        unit(u, h + 1, k + 1, M6, range(DC // 2, DC))

                    head(k, first_half, second_half, lambda: opening(k + 1))
                def first_out(chunks):
                    for c in chunks:
                        if c == 0:
                            pe.wait_ge(*ready(N_WOUT, l))
                            pe.wait_ge(*hd_act.at("p8", l * 4 + 3))
                            pe.wait_ge(*hd_dve.at("tl8_1", l * 4 + 3))
                        pe.wait_ge(*(tail_po.at(f"l{c}", l) if c < 7 else tail_dve.at("l7", l)))
                        for t_ in range(NT):
                            xh, xl = HH[:, c, TW * t_:TW * t_ + TW], HL[:, c, TW * t_:TW * t_ + TW]
                            pe.matmul(A[:, t_, 0:TW], WH[0][:, c, :], xh, start=(c == 0), stop=False)
                            pe.matmul(A[:, t_, 0:TW], WH[0][:, c, :], xl, start=False, stop=False)
                            m = pe.matmul(A[:, t_, 0:TW], WL[0][:, c, :], xh, start=False, stop=(c == DC - 1))
                    return m

                head(l * HEADS + 3, lambda i: None, lambda i: None, lambda: first_out(range(0, 3)))
                first_out(range(3, 7))
                first_out([7]).then_inc(*wo_pe.inc("m0"))
                pe.wait_ge(*hd_dve.at("ob8", l * 4 + 3))
                pe.wait_ge(*ready(N_WOUT + 1, l))
                project(B, 1).then_inc(*wo_pe.inc("m1"))
                pe.sem_inc(past_pe, 1)
                with pe.Fori(1, DC // 2) as m_:
                    for j, ps in enumerate((A, B)):
                        pe.wait_ge(*ready(m_ * 2 + (N_WOUT + j), l))
                        pe.wait_ge(*wo_act.at(f"sq{j}", l * 4 + m_ - 1))
                        project(ps, j).then_inc(*wo_pe.inc(f"m{j}"))
                pe.wait_ge(*wo_dve.at("ss1", l * 4 + 3))
                stat(A, S[2], Wb[0])
                enter(Fe, l, N_UP, up_pe.inc("g0"))
                pe.wait_ge(*Fe[1].at("std2", l))

                def up(g, n, prev):
                    for j in range(G):
                        for e, ps in enumerate((A, B)):
                            if prev == "" and j == 0 and e == 0:
                                continue
                            pe.wait_ge(*ready(n + (2 * j + e), l))
                            kk = l * NG + g
                            if j == 1:
                                pe.wait_ge(*up_dve.at(("ev0", "f0")[e], kk))
                            elif prev == "up":
                                pe.wait_ge(*up_dve.at(("ev1", "f1")[e], kk - 1))
                            elif prev == "down":
                                pe.wait_ge(*dn_dve.at(("a6", "a7")[e], kk - 2))
                            project(ps, e).then_inc(*up_pe.inc(f"{'gv'[e]}{j}"))

                def down(g, n, fs, final=False):
                    kk = l * NG + g
                    slot = 0 if final else 2
                    pe.wait_ge(*ready(n + 1, l))
                    pe.wait_ge(*up_dve.at("fl1", kk))
                    for m in range(DC):
                        ps = (A, B)[m % 2]
                        if m < 2 and not final:
                            pe.wait_ge(*up_dve.at(("ev1", "f1")[m], kk + 1))
                        elif m >= 2:
                            pe.wait_ge(*dn_dve.at(f"a{m - 2}", kk))
                        else:
                            pe.wait_ge(*dn_dve.at(f"a{m + 6}", kk - 1))
                        for t_ in range(NT):
                            for j in range(G):
                                fh = FH[:, fs + j, TW * t_:TW * t_ + TW]
                                fl = FL[:, fs + j, TW * t_:TW * t_ + TW]
                                q = pe.matmul(ps[:, t_, 0:TW], WH[slot + j][:, m, :], fh, start=(j == 0), stop=False)
                                q = pe.matmul(ps[:, t_, 0:TW], WH[slot + j][:, m, :], fl, start=False, stop=False)
                                q = pe.matmul(ps[:, t_, 0:TW], WL[slot + j][:, m, :], fh, start=False, stop=(j == G - 1))
                        q.then_inc(*dn_pe.inc(f"m{m}"))

                last = NG - 1
                up(0, N_UP, "")
                up(1, N_UP + 4, "up")
                down(0, N_UP + 8, 0)
                with pe.Fori(1, NG // 2) as g2:
                    g = g2 * 2
                    up(g, g * 6 + (N_UP - 2), "down")
                    down(g - 1, g * 6 + (N_UP + 2), 2)
                    up(g + 1, g * 6 + (N_UP + 4), "down")
                    down(g, g * 6 + (N_UP + 8), 0)
                down(last, N_UP + 6 * NG - 2, 2, final=True)
                pe.wait_ge(*ps_dve.at("ss7", l))
                pe.wait_ge(*dn_dve.at("a7", l * NG + last))
                stat(A, CH[4], Fb[0])
            for e in range(2):
                pe.wait_ge(*Fb[3].at(f"hn{4 * e + 3}", L - 1))
                for b in range(8):
                    if e == 1:
                        pe.wait_ge(ep_act, b + 1)
                    for c in range(4):
                        t0 = META + P * b
                        m = pe.transpose(EIGHT[b][:, c * P:(c + 1) * P], ACC[:, 4 * e + c, t0:t0 + P], IDENT[:, 0:P])
                    m.then_inc(ep_pe, 1)

        @block.scalar
        def _(ac):
            def act(dst, src, f, **kw):
                return nc.scalar.activation(dst, src, f, **kw)

            def std(dst, ps, width, eps, l, sums, marks):
                for t_ in range(NT):
                    ac.wait_ge(*sums.at(STAT[t_], l))
                    act(dst[:, TW * t_:TW * t_ + TW], ps[:, t_, 0:TW], ACT.Sqrt, scale=1.0 / width,
                        bias=eps).then_inc(*marks.inc(STD[t_]))

            ahead(ac, "act")

            def tokens(b):
                rows, ps = (META if b == 0 else P), (A, B)[b % 2]
                t0 = 0 if b == 0 else META + P * (b - 1)
                src = ps[:, 0:2, :].rearrange("p a b -> p (a b)").rearrange("p (c t) -> p c t", t=P)[:, :, 0:rows]
                ac.wait_ge(x_pe, b + 1)
                act(ACC[:, :, t0:t0 + rows], src, ACT.Copy).then_inc(x_act, 1)

            for b in range(6):
                tokens(b)
            ac.wait_ge(start_dve, 4)
            ac.wait_ge(start_pe, 2)
            act(SM[:, 8:8 + 2 * L], M7[:, 0:2 * L], ACT.Exp).then_inc(start_act, 1)
            ac.wait_ge(start_dve, 6)
            act(SM[:, 24:32], SM[:, 16:24], ACT.Exp, scale=-1.0).then_inc(start_act, 1)
            for b in range(6, 9):
                tokens(b)

            with ac.Fori(0, L) as l:
                def enter(E, new):
                    for c in range(DC):
                        ac.wait_ge(*new.at(f"hn{c}", l - (E is Me)))
                        if c == 0 and E is Me:
                            ac.wait_ge(x_act, 9)
                        act(HH[:, c, :], ACC[:, c, :], ACT.Copy).then_inc(*E[1].inc(f"hh{c}"))
                        if c >= 2:
                            ac.wait_ge(*E[0].at(f"st{c - 2}", l))
                        act(S[c % 2][:, 0:T], ACC[:, c, :], ACT.Square).then_inc(*E[1].inc(f"sq{c}"))
                    std(RSTD, B, D, EPS_D, l, E[0], E[1])

                enter(Me, Fb[3])
                with ac.Fori(0, LRU_CH) as c:
                    k = l * LRU_CH + c
                    ac.wait_ge(*lru_dve.at("xev", k))
                    act(XC[:, :], XPAD[:, 3:3 + T], ACT.Identity, scale=col(c + (CONV_W + 12)),
                        bias=col(c + CONV_B)).then_inc(*lru_act.inc("c3"))
                    ac.wait_ge(*lru_dve.at("c0", k))
                    act(XH[:, :], XC[:, :], ACT.Copy).then_inc(*lru_act.inc("xch"))
                    ac.wait_ge(*lru_dve.at("gev", k))
                    act(GG[:, :], GG[:, :], ACT.Gelu_apprx_tanh).then_inc(*lru_act.inc("gg"))
                    ac.wait_ge(*lru_pe.at("r", k))
                    act(tt(RA[:, :]), AT, ACT.Sigmoid, bias=col(c + GATE_BA)).then_inc(*lru_act.inc("r"))
                    ac.wait_ge(*lru_pe.at("i", k))
                    act(tt(IB[:, :]), BT, ACT.Sigmoid, bias=col(c + GATE_BX)).then_inc(*lru_act.inc("i"))
                    ac.wait_ge(*lru_act.at("r", k))
                    ac.wait_ge(*lru_dve.at("ss", k - 1))
                    act(S[1][:, 0:T], RA[:, :], ACT.Tanh, scale=col(c + NEG_C)).then_inc(*lru_act.inc("t"))
                    ac.wait_ge(*lru_act.at("t", k))
                    act(RA[:, :], RA[:, :], ACT.Exp, scale=col(c + POS_C)).then_inc(*lru_act.inc("a"))
                    ac.wait_ge(*lru_dve.at("m2", k))
                    act(S[0][:, 0:T], S[0][:, 0:T], ACT.Sqrt).then_inc(*lru_act.inc("m"))

                def swap(u, k, xyz=XYZ):
                    ac.wait_ge(*pj_dve.at(f"sn{u}", k))
                    for j in range(4):
                        a, b = 32 * j, 32 * (j ^ 1)
                        act(xyz[a:a + 32, 2, :], xyz[b:b + 32, 1, :], ACT.Copy).then_inc(*pj_act.inc(f"z{u}_{j}"))

                def split_qk(k):
                    ac.wait_ge(*pj_po.at("ad5", k))
                    ac.wait_ge(*hd_pe.at("s8b", k - 1))
                    act(QKH[:, 0, :], QKN[:, 0, :], ACT.Copy).then_inc(*qk_act.inc("qh"))
                    act(QKH[:, 1, :], QKN[:, 1, :], ACT.Copy).then_inc(*qk_act.inc("kh"))

                def exp(i, mp, k):
                    keys, c0 = META + P * i, columns(i)[0]
                    ps, dst = (AF, BFL)[mp], (S[i % 2], S[2])[mp]
                    ac.wait_ge(*hd_dve.at(f"{('nb', 'nc')[mp]}{i}", k))
                    if mp == 1 and i >= 1:
                        ac.wait_ge(*hd_dve.at(f"x{i - 1}", k))
                    if mp == 0 and i == 1:
                        ac.wait_ge(*ln_dve.at("y3", l))
                    if mp == 0 and i >= 2:
                        ac.wait_ge(*hd_pe.at(f"t{i - 2}_{len(rounds(i - 2)) - 1}", k))
                    act(dst[:, 0:keys], ps[:, c0:c0 + keys], ACT.Exp, scale=DH ** -0.5, bias=SM[:, 34 + mp:35 + mp],
                        accum_out=SM[:, 36 + mp + 2 * (i % 2):37 + mp + 2 * (i % 2)]
                        ).then_inc(*hd_act.inc(f"{'pq'[mp]}{i}"))

                def opening(k):
                    exp(0, 0, k)
                    exp(0, 1, k)
                    ac.wait_ge(*hd_pe.at("vt", k))
                    ac.wait_ge(*hd_pe.at("pv8", k - 1))
                    act(VV[:, 1:NQ, 0, :], AF[:, 512:512 + 8 * P].rearrange("p (a b) -> p a b", b=P),
                        ACT.Copy).then_inc(*hd_act.inc("vh"))
                    ac.wait_ge(*hd_dve.at("vz", k))
                    act(VV[0:META, 0, 0, :], B[0:META, 1, 0:P], ACT.Copy).then_inc(*hd_act.inc("vm"))

                def head(row, k, swaps, following, last):
                    def turned(i, r):
                        ac.wait_ge(*hd_pe.at(f"t{i}_{r}", k))
                        if i >= 1 and r == 0:
                            ac.wait_ge(*hd_pe.at(f"pv{i - 1}", k))
                        b, ps = rounds(i)[r], (M7, A[:, 0, :], M7)[r]
                        act(PTH[:, b[0]:b[0] + len(b), :], ps[:, 0:len(b) * P].rearrange("p (a b) -> p a b", b=P),
                            ACT.Copy).then_inc(*hd_act.inc(f"th{i}_{r}"))

                    def out_hi(i):
                        ac.wait_ge(*hd_pe.at(f"pv{i}", k))
                        ac.wait_ge(*(hd_pe.at(f"ot{i - 2}", k) if i >= 2 else hd_pe.at("ot8", k - 1)))
                        rs = 40 + 2 * (i % 2)
                        act(OT[i % 2][:, :], B[:, 0, 0:P], ACT.Copy, scale=SM[:, rs:rs + 1]).then_inc(*hd_act.inc(f"oa{i}"))

                    def out_square(i):
                        ac.wait_ge(*hd_dve.at(f"ob{i}", k))
                        act(OSQ[:, :], OT[i % 2][:, :], ACT.Square, accum_out=SM[:, 46 + i % 2:47 + i % 2]
                            ).then_inc(*hd_act.inc(f"sq{i}"))

                    def out(i):
                        ac.wait_ge(*hd_pe.at(f"ot{i}", k))
                        q0, qn = (0, META) if i == 0 else (META + P * (i - 1), P)
                        act(ACC[:, bass.ds(row, 1), q0:q0 + qn].rearrange("p a b -> p (a b)"), M7[:, 3 * P:3 * P + qn],
                            ACT.Copy, scale=col(HEAD_GAIN)).then_inc(*hd_act.inc(f"oc{i}"))

                    for i in range(NQ):
                        n, nr, more = i + 1, len(rounds(i)), i + 1 < NQ
                        turned(i, 0)
                        if nr > 1:
                            turned(i, 1)
                        if i:
                            out_hi(i - 1)
                        if more:
                            exp(n, 0, k)
                        if nr > 2:
                            turned(i, 2)
                        if i:
                            out_square(i - 1)
                        if more:
                            exp(n, 1, k)
                        if i >= 2:
                            out(i - 2)
                        swaps(i)
                    out_hi(8)
                    out_square(8)
                    following()
                    out(7)
                    out(8)
                    last()

                for u in range(6):
                    swap(u, l * 4, (XYZ, XYZ0)[u % 2])
                    if u == 4:
                        std(S[1], A, 512, EPS_D, l, ln_pe, ln_act)
                split_qk(l * 4)
                opening(l * HEADS)
                with ac.Fori(0, HEADS - 1) as h:
                    k = l * HEADS + h

                    def swaps(i):
                        if 1 <= i <= 6:
                            swap(i - 1, k + 1)
                        elif i == 8:
                            split_qk(k + 1)

                    head(h + 4, k, swaps, lambda: opening(k + 1), lambda: None)

                def split_chunk(c):
                    ac.wait_ge(*pj_pe.at("u8", l * 4 + 3))
                    if c >= 4:
                        ac.wait_ge(*hd_act.at("oc8", l * 4 + c - 4))
                    act(HH[:, c, :], ACC[:, c, :], ACT.Copy).then_inc(*tail_act.inc(f"h{c}"))

                head(7, l * HEADS + 3, lambda i: split_chunk(i - 1) if 1 <= i <= 7 else None, lambda: None,
                     lambda: split_chunk(7))
                with ac.Fori(0, DC // 2) as m:
                    for j, ps in enumerate((AT, BT)):
                        kk = l * 4 + m
                        ac.wait_ge(*wo_pe.at(f"m{j}", kk))
                        act(ACC[:, bass.ds(m * 2 + j, 1), :].rearrange("p x (a b) -> p (x a) b", a=NT), ps,
                            ACT.Copy).then_inc(*wo_act.inc(f"y{j}"))
                        ac.wait_ge(*wo_dve.at(f"ss{j}", kk - 1))
                        act(tt(S[j][:, 0:T]), ps, ACT.Square).then_inc(*wo_act.inc(f"sq{j}"))

                def post(Bd, r2):
                    std(r2, A, D, EPS_D, l, Bd[0], Bd[1])

                post(Wb, S[3])
                enter(Fe, Wb[3])

                def gate(g, fs):
                    kk = l * NG + g
                    for j in range(G):
                        ac.wait_ge(*up_dve.at(f"ev{j}", kk))
                        act(S[1][:, 0:T], S[0][:, 2:2 + T], ACT.Identity, scale=col(g * 2 + (FCONV_W + 48 + j)),
                            bias=col(g * 2 + (FCONV_B + j))).then_inc(*up_act.inc(f"c2{j}"))
                        ac.wait_ge(*up_dve.at(f"c0{j}", kk))
                        act(S[2][:, 0:T], S[1][:, 0:T], ACT.Gelu_apprx_tanh).then_inc(*up_act.inc(f"ge{j}"))
                        ac.wait_ge(*up_dve.at(f"f{j}", kk))
                        ac.wait_ge(*dn_pe.at("m7", kk - 2))
                        act(FH[:, fs + j, :], S[3][:, 0:T], ACT.Copy).then_inc(*up_act.inc(f"fh{j}"))

                with ac.Fori(0, NG // 2) as g2:
                    gate(g2 * 2, 0)
                    gate(g2 * 2 + 1, 2)
                for m in range(DC):
                    ac.wait_ge(*dn_dve.at(f"a{m}", l * NG + NG - 1))
                    if m >= 2:
                        ac.wait_ge(*ps_dve.at(f"ss{m - 2}", l))
                    act(CH[m % 2][:, :], ACC[:, m, :], ACT.Square).then_inc(*ps_act.inc(f"sq{m}"))
                post(Fb, CH[5])
            ac.wait_ge(*fr_po.at("r7", L - 1))
            for e in range(2):
                for b in range(8):
                    ac.wait_ge(ep_pe, 8 * e + b + 1)
                    act(OUTB[:, b, 512 * e:512 * e + 512], EIGHT[b][:, 0:512], ACT.Copy).then_inc(ep_act, 1)

        @block.vector
        def _(dv):
            v = nc.vector
            ahead(dv, "dve")

            def flat(ap):
                return ap.rearrange("p a b -> p (a b)")

            def inverse(r, l, stds, marks):
                for t_ in range(NT):
                    dv.wait_ge(*stds.at(STD[t_], l))
                    tile = r[:, TW * t_:TW * t_ + TW]
                    v.reciprocal(tile, tile).then_inc(*marks.inc(INV[t_]))

            v.memset(EPS_D, 1e-6)
            v.memset(MINUS_HALF, -0.5)
            v.memset(HEAD_EPS, P * 1e-5)
            v.memset(ONE, 1.0).then_inc(start_dve, 1)
            v.memset(PAR[:, L, :], 0.0)
            v.memset(ACC[:, :, TOK:T], 0.0)
            dv.wait_ge(start_pe, 1)
            v.tensor_copy(PAR[:, 0:L, :], M6[:, :].rearrange("p (l n) -> p l n", l=L)).then_inc(start_dve, 1)
            dv.wait_ge(start_dve, 2)
            v.tensor_tensor(SM[:, 0:2 * L].rearrange("p (l n) -> p l n", l=L), PAR[:, 0:L, LAM:LAM + 2],
                            PAR[:, 0:L, LAM + 2:LAM + 4], ALU.mult).then_inc(start_dve, 1)
            v.tensor_scalar(SM[:, 16:24].rearrange("p (l n) -> p l n", l=L), PAR[:, 0:L, A_PAR:A_PAR + 4], -1.0, None,
                            ALU.mult).then_inc(start_dve, 1)
            dv.wait_ge(start_dve, 4)
            am = SM[:, 32:40]
            v.tensor_scalar(am.rearrange("p (l n) -> p l n", l=L), PAR[:, 0:L, A_PAR:A_PAR + 4], 0.0, None,
                            ALU.min).then_inc(start_dve, 1)
            v.tensor_tensor(SM[:, 16:24].rearrange("p (l n) -> p l n", l=L), PAR[:, 0:L, A_PAR:A_PAR + 4],
                            SM[:, 16:24].rearrange("p (l n) -> p l n", l=L), ALU.max).then_inc(start_dve, 1)
            n = [6]

            def link(ins):
                n[0] += 1
                ins.then_inc(start_dve, 1)
                dv.wait_ge(start_dve, n[0])

            dv.wait_ge(start_act, 2)
            e, w, w2, p = SM[:, 24:32], SM[:, 40:48], SM[:, 48:56], SM[:, 56:64]
            link(v.tensor_scalar(w, e, 2.0, None, ALU.add))
            link(v.reciprocal(w, w))
            link(v.tensor_tensor(w, w, e, ALU.mult))
            link(v.tensor_tensor(w2, w, w, ALU.mult))
            link(v.tensor_scalar(p, w2, 1.0 / 19, 1.0 / 17, ALU.mult, ALU.add))
            for q in (15, 13, 11, 9, 7, 5, 3, 1):
                link(v.tensor_tensor(p, p, w2, ALU.mult))
                link(v.tensor_scalar(p, p, 1.0 / q, None, ALU.add))
            link(v.tensor_tensor(p, p, w, ALU.mult))
            link(v.scalar_tensor_tensor(out=p, in0=p, scalar=-2.0, in1=am, op0=ALU.mult, op1=ALU.add))
            pl = p.rearrange("p (l n) -> p l n", l=L)
            link(v.tensor_scalar(PAR[:, 0:L, POS_C:POS_C + 4], pl, 8.0, None, ALU.mult))
            link(v.tensor_scalar(PAR[:, 0:L, NEG_C:NEG_C + 4], pl, -8.0, None, ALU.mult))
            for l in range(L):
                li = LAMBDA_INIT[l]
                link(v.tensor_tensor(PAR[:, l, NEG_LAM:NEG_LAM + 1], SM[:, 9 + 2 * l:10 + 2 * l],
                                     SM[:, 8 + 2 * l:9 + 2 * l], ALU.subtract))
                link(v.tensor_scalar(PAR[:, l, NEG_LAM:NEG_LAM + 1], PAR[:, l, NEG_LAM:NEG_LAM + 1], -li, None, ALU.add))
                link(v.tensor_scalar(PAR[:, l, HEAD_GAIN:HEAD_GAIN + 1], PAR[:, l, SUBLN:SUBLN + 1], 1.0 - li, None,
                                     ALU.mult))
            v.tensor_copy(CUR[:, :], PAR[:, 0, :]).then_inc(cur_ready, 1)
            dv.wait_ge(x_pe, 9)

            R = RSTD[:, 0:T]
            with dv.Fori(0, L) as l:
                dv.wait_ge(*Fb[3].at("hn7", l - 1))
                v.tensor_copy(GP[:, :], PAR[:, bass.ds(l, 1), FFN_POST:FFN_POST + DC].rearrange("p a b -> p (a b)")
                              ).then_inc(*gp_dve.inc("copy"))
                v.memset(S[2][:, 0:T], 0.0).then_inc(*ln_dve.inc("zero"))
                dv.wait_ge(cur_ready, l + 1)

                def enter(E):
                    inverse(R, l, E[1], E[3])
                    dv.wait_ge(*E[3].at("rstd2", l))

                enter(Me)
                dv.wait_ge(*ln_dve.at("zero", l))
                dv.sem_inc(past_dve, 1)
                with dv.Fori(0, LRU_CH) as c:
                    k = l * LRU_CH + c
                    D_ = lambda nm: dv.wait_ge(*lru_dve.at(nm, k))
                    v.memset(XPAD[:, 0:3], 0.0).then_inc(*lru_dve.inc("pad"))
                    dv.wait_ge(*lru_pe.at("x", k))
                    v.tensor_tensor(tt(XPAD[:, 3:3 + T]), AT, tt(R), ALU.mult).then_inc(*lru_dve.inc("xev"))
                    dv.wait_ge(*lru_act.at("c3", k))
                    for j, nm in ((2, "c2"), (1, "c1"), (0, "c0")):
                        D_({2: "xev", 1: "c2", 0: "c1"}[j])
                        v.scalar_tensor_tensor(out=XC[:, :], in0=XPAD[:, j:j + T], scalar=col(c + (CONV_W + 4 * j)),
                                               in1=XC[:, :], op0=ALU.mult, op1=ALU.add).then_inc(*lru_dve.inc(nm))
                    dv.wait_ge(*lru_act.at("xch", k))
                    v.tensor_tensor(XL[:, :], XC[:, :], XH[:, :].bitcast(F32), ALU.subtract).then_inc(*lru_dve.inc("xcl"))
                    dv.wait_ge(*lru_pe.at("g", k))
                    v.tensor_tensor(tt(GG[:, :]), BT, tt(R), ALU.mult).then_inc(*lru_dve.inc("gev"))
                    dv.wait_ge(*lru_act.at("i", k))
                    v.tensor_tensor(IB[:, :], IB[:, :], XC[:, :], ALU.mult).then_inc(*lru_dve.inc("ix"))
                    dv.wait_ge(*lru_act.at("a", k))
                    s0, s1 = S[0][:, 0:T], S[1][:, 0:T]
                    v.tensor_tensor(s0, RA[:, :], RA[:, :], ALU.mult).then_inc(*lru_dve.inc("a2"))
                    D_("a2")
                    v.scalar_tensor_tensor(out=s0, in0=s0, scalar=1.0, in1=s1, op0=ALU.add,
                                           op1=ALU.mult).then_inc(*lru_dve.inc("m2"))
                    dv.wait_ge(*lru_act.at("m", k))
                    D_("ix")
                    v.tensor_tensor(IB[:, :], IB[:, :], s0, ALU.mult).then_inc(*lru_dve.inc("b"))
                    D_("b")
                    v.tensor_tensor_scan(s1, RA[:, :], IB[:, :], 0.0, ALU.mult, ALU.add).then_inc(*lru_dve.inc("scan"))
                    D_("scan")
                    dv.wait_ge(res_out, l * 16 + 16)
                    y = flat(ACC[:, bass.ds(c, 1), :])
                    v.tensor_tensor(y, s1, GG[:, :], ALU.mult).then_inc(*lru_dve.inc("y"))
                    D_("y")
                    v.tensor_tensor(s0, y, y, ALU.mult).then_inc(*lru_dve.inc("sq"))
                    D_("sq")
                    v.tensor_tensor(S[2][:, 0:T], S[2][:, 0:T], s0, ALU.add).then_inc(*lru_dve.inc("ss"))

                def unit(u, k, ps=M6, xyz=XYZ, back=1):
                    tl = slice(TW * (u % 3), TW * (u % 3) + TW)
                    dv.wait_ge(*pj_pe.at(f"u{u}", k))
                    if u == 6:
                        dv.wait_ge(*hd_pe.at("vt", k - 1))
                    elif u < 6:
                        dv.wait_ge(*(pj_po.at(f"ad{u - back}", k) if u >= back else pj_po.at("ad5", k - 1)))
                    dst = xyz[:, 0, :] if u < 6 else VN[:, tl]
                    v.tensor_tensor(dst, ps[:, 0:TW], RSTD[:, tl], ALU.mult).then_inc(*pj_dve.inc(f"ev{u}"))
                    if u < 6:
                        dv.wait_ge(*pj_dve.at(f"ev{u}", k))
                        v.tensor_tensor(xyz[:, 1, :], xyz[:, 0, :], SIN[:, tl], ALU.mult).then_inc(*pj_dve.inc(f"sn{u}"))

                dv.wait_ge(const_in, 32)
                dv.wait_ge(*lru_dve.at("ss", l * LRU_CH + 3))
                for u in range(9):
                    unit(u, l * 4, BANKS[u], (XYZ, XYZ0)[u % 2], 2)
                    if u == 6:
                        inverse(S[1], l, ln_act, ln_dve)

                def split_qk(k):
                    for e, x in enumerate("qk"):
                        dv.wait_ge(*qk_act.at(f"{x}h", k))
                        v.tensor_tensor(QKL[:, e, :], QKN[:, e, :], QKH[:, e, :].bitcast(F32),
                                        ALU.subtract).then_inc(*qk_dve.inc(f"{x}l"))

                def maximum(i, mp, k):
                    keys, c0 = META + P * i, columns(i)[0]
                    mx, nb = (("mx", "nb"), ("my", "nc"))[mp]
                    dv.wait_ge(*hd_pe.at(f"s{i}{'ab'[mp]}", k))
                    v.tensor_reduce(SM[:, 32 + mp:33 + mp], (AF, BFL)[mp][:, c0:c0 + keys], AX_X,
                                    ALU.max).then_inc(*hd_dve.inc(f"{mx}{i}"))
                    dv.wait_ge(*hd_dve.at(f"{mx}{i}", k))
                    v.tensor_scalar(SM[:, 34 + mp:35 + mp], SM[:, 32 + mp:33 + mp], -(DH ** -0.5), None,
                                    ALU.mult).then_inc(*hd_dve.inc(f"{nb}{i}"))

                def combine(i, k):
                    keys = META + P * i
                    p1, p2 = S[i % 2][:, 0:keys], S[2][:, 0:keys]
                    sm, rs = 36 + 2 * (i % 2), 40 + 2 * (i % 2)
                    dv.wait_ge(*hd_act.at(f"q{i}", k))
                    v.reciprocal(SM[:, rs:rs + 2], SM[:, sm:sm + 2]).then_inc(*hd_dve.inc(f"r{i}"))
                    dv.wait_ge(*hd_dve.at(f"r{i}", k))
                    v.scalar_tensor_tensor(out=SM[:, 44:45], in0=SM[:, sm:sm + 1], scalar=col(NEG_LAM),
                                           in1=SM[:, rs + 1:rs + 2], op0=ALU.mult, op1=ALU.mult
                                           ).then_inc(*hd_dve.inc(f"u{i}"))
                    dv.wait_ge(*hd_dve.at(f"u{i}", k))
                    v.scalar_tensor_tensor(out=p1, in0=p2, scalar=SM[:, 44:45], in1=p1, op0=ALU.mult,
                                           op1=ALU.add).then_inc(*hd_dve.inc(f"x{i}"))

                def opening(k, between):
                    maximum(0, 0, k)
                    maximum(0, 1, k)
                    dv.wait_ge(*hd_pe.at("pv8", k - 1))
                    v.memset(VV[:, 0, :, :].bitcast(F32), 0.0).then_inc(*hd_dve.inc("vz"))
                    between()
                    combine(0, k)
                    v.memset(S[0][:, META:P], 0.0).then_inc(*hd_dve.inc("z0"))
                    dv.wait_ge(*hd_act.at("vh", k))
                    v.tensor_tensor(VV[:, 1:NQ, 1, :], AF[:, 512:512 + 8 * P].rearrange("p (a b) -> p a b", b=P),
                                    VV[:, 1:NQ, 0, :].bitcast(F32), ALU.subtract).then_inc(*hd_dve.inc("vl"))
                    dv.wait_ge(*hd_dve.at("vz", k))
                    dv.wait_ge(*hd_act.at("vm", k))
                    v.tensor_tensor(VV[0:META, 0, 1, :], B[0:META, 1, 0:P], VV[0:META, 0, 0, :].bitcast(F32),
                                    ALU.subtract).then_inc(*hd_dve.inc("vm"))

                def head(k, units, following):
                    def turned(i, r):
                        dv.wait_ge(*hd_act.at(f"th{i}_{r}", k))
                        b, ps = rounds(i)[r], (M7, A[:, 0, :], M7)[r]
                        b0, nb = b[0], len(b)
                        dst = PTLB[:, b0 - 3:b0 - 3 + nb, :] if b0 >= 3 else PTLA[:, b0:b0 + nb, :]
                        v.tensor_tensor(dst, ps[:, 0:nb * P].rearrange("p (a b) -> p a b", b=P),
                                        PTH[:, b0:b0 + nb, :].bitcast(F32), ALU.subtract).then_inc(*hd_dve.inc(f"tl{i}_{r}"))

                    def out_lo(i):
                        dv.wait_ge(*hd_act.at(f"oa{i}", k))
                        rs = 40 + 2 * (i % 2)
                        v.scalar_tensor_tensor(out=OT[i % 2][:, :], in0=B[:, 0, P:2 * P], scalar=SM[:, rs:rs + 1],
                                               in1=OT[i % 2][:, :], op0=ALU.mult, op1=ALU.add
                                               ).then_inc(*hd_dve.inc(f"ob{i}"))

                    def out_norm(i):
                        e = i % 2
                        dv.wait_ge(*hd_po.at(f"rn{i}", k))
                        v.tensor_scalar(OT[e][:, :], OT[e][:, :], SM[:, 48 + e:49 + e], float(P) ** 0.5, ALU.mult,
                                        ALU.mult).then_inc(*hd_dve.inc(f"sc{i}"))

                    for i in range(NQ):
                        n, nr, more = i + 1, len(rounds(i)), i + 1 < NQ
                        turned(i, 0)
                        if nr > 1:
                            turned(i, 1)
                        if more:
                            maximum(n, 0, k)
                        if i:
                            out_lo(i - 1)
                        if nr > 2:
                            turned(i, 2)
                        if more:
                            maximum(n, 1, k)
                        if i >= 2:
                            out_norm(i - 2)
                        if more:
                            combine(n, k)
                        units(i)
                    out_lo(8)
                    out_norm(7)
                    following(lambda: out_norm(8))

                split_qk(l * 4)
                opening(l * HEADS, lambda: None)
                dv.wait_ge(*ln_dve.at("rstd2", l))
                for c in range(LRU_CH):
                    v.scalar_tensor_tensor(out=ACC[:, c, :], in0=ACC[:, c, :], scalar=col(OUT_NORM + c), in1=S[1][:, 0:T],
                                           op0=ALU.mult, op1=ALU.mult).then_inc(*ln_dve.inc(f"y{c}"))
                with dv.Fori(0, HEADS - 1) as h:
                    k = l * HEADS + h

                    def units(i):
                        if i == 8:
                            split_qk(k + 1)
                        unit(i, k + 1)

                    head(k, units, lambda between: opening(k + 1, between))

                head(l * HEADS + 3, lambda i: None, lambda between: between())
                v.memset(S[2][:, 0:T], 0.0).then_inc(*tail_dve.inc("zero"))
                dv.wait_ge(*tail_act.at("h7", l))
                v.tensor_tensor(HL[:, 7, :], ACC[:, 7, :], HH[:, 7, :].bitcast(F32),
                                ALU.subtract).then_inc(*tail_dve.inc("l7"))
                with dv.Fori(0, DC // 2) as m:
                    for j in range(2):
                        kk = l * 4 + m
                        dv.wait_ge(*wo_act.at(f"sq{j}", kk))
                        dv.wait_ge(*(wo_dve.at("ss1", kk - 1) if j == 0 else wo_dve.at("ss0", kk)))
                        v.tensor_tensor(S[2][:, 0:T], S[2][:, 0:T], S[j][:, 0:T], ALU.add).then_inc(*wo_dve.inc(f"ss{j}"))

                def mix(Bd, r2, gain, res, ready_):
                    inverse(r2, l, Bd[1], Bd[2])
                    dv.wait_ge(*Bd[2].at("rstd2", l))
                    for c in range(DC):
                        a = ACC[:, c, :]
                        v.scalar_tensor_tensor(out=a, in0=a, scalar=gain(c), in1=r2, op0=ALU.mult,
                                               op1=ALU.mult).then_inc(*Bd[3].inc(f"t{c}"))
                        dv.wait_ge(*Bd[3].at(f"t{c}", l))
                        if ready_:
                            dv.wait_ge(*ready_.at(f"r{c}", l))
                        v.tensor_tensor(a, a, res(c), ALU.add).then_inc(*Bd[3].inc(f"hn{c}"))

                dv.wait_ge(res_in, l * 16 + 16)
                mix(Wb, S[3][:, 0:T], lambda c: col(MIX_POST + c), lambda c: HRES[:, c, :], None)
                enter(Fe)

                def up(g, fs):
                    kk = l * NG + g
                    D_ = lambda nm: dv.wait_ge(*up_dve.at(nm, kk))
                    s1, s2, s3 = S[1][:, 0:T], S[2][:, 0:T], S[3][:, 0:T]
                    for j in range(G):
                        v.memset(S[0][:, 0:2], 0.0).then_inc(*up_dve.inc(f"pad{j}"))
                        dv.wait_ge(*up_pe.at(f"g{j}", kk))
                        v.tensor_tensor(tt(S[0][:, 2:2 + T]), AT, tt(R), ALU.mult).then_inc(*up_dve.inc(f"ev{j}"))
                        dv.wait_ge(*up_act.at(f"c2{j}", kk))
                        D_(f"ev{j}")
                        for q, nm, prev in ((1, "c1", "ev"), (0, "c0", "c1")):
                            D_(f"{prev}{j}")
                            v.scalar_tensor_tensor(out=s1, in0=S[0][:, q:q + T], scalar=col(g * 2 + (FCONV_W + 24 * q + j)),
                                                   in1=s1, op0=ALU.mult, op1=ALU.add).then_inc(*up_dve.inc(f"{nm}{j}"))
                        dv.wait_ge(*up_act.at(f"ge{j}", kk))
                        v.tensor_tensor(s2, s2, R, ALU.mult).then_inc(*up_dve.inc(f"gr{j}"))
                        D_(f"gr{j}")
                        dv.wait_ge(*up_pe.at(f"v{j}", kk))
                        v.tensor_tensor(tt(s3), tt(s2), BT, ALU.mult).then_inc(*up_dve.inc(f"f{j}"))
                        dv.wait_ge(*up_act.at(f"fh{j}", kk))
                        v.tensor_tensor(FL[:, fs + j, :], s3, FH[:, fs + j, :].bitcast(F32),
                                        ALU.subtract).then_inc(*up_dve.inc(f"fl{j}"))

                def down(g, first=False):
                    kk = l * NG + g
                    for m in range(DC):
                        ps, a = (AT, BT)[m % 2], ACC[:, m, :].rearrange("p (a b) -> p a b", a=NT)
                        dv.wait_ge(*dn_pe.at(f"m{m}", kk))
                        if first:
                            v.tensor_copy(a, ps).then_inc(*dn_dve.inc(f"a{m}"))
                        else:
                            dv.wait_ge(*dn_dve.at(f"a{m}", kk - 1))
                            v.tensor_tensor(a, a, ps, ALU.add).then_inc(*dn_dve.inc(f"a{m}"))

                up(0, 0)
                up(1, 2)
                down(0, first=True)
                with dv.Fori(1, NG // 2) as g2:
                    up(g2 * 2, 0)
                    down(g2 * 2 - 1)
                    up(g2 * 2 + 1, 2)
                    down(g2 * 2)
                v.tensor_copy(CUR[:, :], flat(PAR[:, bass.ds(l + 1, 1), :])).then_inc(cur_ready, 1)
                ssl = CH[4][:, :]
                v.memset(ssl, 0.0).then_inc(*ps_dve.inc("zero"))
                kk = l * NG + NG - 1
                for m in range(DC + 1):
                    if m < DC:
                        dv.wait_ge(*dn_pe.at(f"m{m}", kk))
                        a = ACC[:, m, :].rearrange("p (a b) -> p a b", a=NT)
                        dv.wait_ge(*dn_dve.at(f"a{m}", kk - 1))
                        v.tensor_tensor(a, a, (AT, BT)[m % 2], ALU.add).then_inc(*dn_dve.inc(f"a{m}"))
                    if m >= 1:
                        dv.wait_ge(*ps_act.at(f"sq{m - 1}", l))
                        dv.wait_ge(*ps_dve.at("zero" if m == 1 else f"ss{m - 2}", l))
                        v.tensor_tensor(ssl, ssl, CH[(m - 1) % 2][:, :], ALU.add).then_inc(*ps_dve.inc(f"ss{m - 1}"))
                mix(Fb, CH[5][:, :], lambda c: GP[:, c:c + 1], lambda c: HSUM[:, c, :], fr_po)


LAMBDA_INIT = [0.8 - 0.6 * 2.718281828459045 ** (-0.3 * l) for l in range(L)]

NAMES = ["x", "meta_tokens", "ln_mix_pre", "ln_mix_post", "ln_ffn_pre", "ln_ffn_post", "w_in", "lru_conv_w",
         "lru_conv_b", "lru_wa", "lru_ba", "lru_wx", "lru_bx", "lru_a_param", "lru_out_norm", "lam_q1", "lam_k1",
         "lam_q2", "lam_k2", "diff_subln", "w_out", "w_up", "ffn_conv_w", "ffn_conv_b", "w_down"]


def rope_tables():
    import numpy as np
    inv = 1.0 / (np.float32(10000.0) ** (np.arange(0, DH, 2, dtype=np.float32) / np.float32(DH)))
    ang = inv.astype(np.float32)[:, None] * np.arange(T, dtype=np.float32)[None, :]
    cos, sin = np.cos(ang).astype(np.float32), np.sin(ang).astype(np.float32)
    return np.tile(cos, (4, 1)), np.concatenate([sin, -sin, sin, -sin], 0)


def kernel(**inputs):
    import numpy as np
    import concourse.bacc as bacc
    from concourse.bass_utils import run_bass_kernel_spmd

    nc = bacc.Bacc("TRN2", target_bir_lowering=False, num_devices=1)
    cos, sin = rope_tables()
    arrays = {n: np.ascontiguousarray(inputs[n]) for n in NAMES}
    arrays |= {"cos": cos, "sin": sin}
    t = {n: nc.dram_tensor(f"in_{n}", a.shape, F32, kind="ExternalInput").ap() for n, a in arrays.items()}
    t["stream"] = nc.dram_tensor("stream", (P, DC * T), F32, kind="Internal").ap()
    out = nc.dram_tensor("out", (1, SEQ, D), F32, kind="ExternalOutput").ap()
    trunk(nc, t, out)
    r = run_bass_kernel_spmd(nc, [{f"in_{n}": a for n, a in arrays.items()}], core_ids=[0])
    return r.results[0]["out"]
```
